# Optimizing a Trainium2 kernel written in Bass

```python
import math
import jax, jax.numpy as jnp
from jax import lax
import numpy as np

D_MODEL = 1024
BATCH = 1
SEQ = 256
DEPTH = 1

SB_WIDTH = D_MODEL // 2
SB_HEAD_DIM = 64
SB_HEADS = SB_WIDTH // SB_HEAD_DIM
SB_BLOCK = 128
HGRN_WIDTH = D_MODEL // 2
HGRN_HEAD_DIM = 128
HGRN_HEADS = HGRN_WIDTH // HGRN_HEAD_DIM
HGRN_CHUNK = 64
N_EXPERTS = 32
TOP_K = 4
D_FF = D_MODEL
SWIGLU_ALPHA = 1.702
SWIGLU_LIMIT = 7.0
EXPERT_BLOCK = 128
DEEPNORM_ALPHA = (2 * DEPTH) ** 0.25
DEEPNORM_BETA = (8 * DEPTH) ** -0.25
LN_EPS = 1e-5
RMS_EPS = 1e-6
IN_SPLITS = (SB_WIDTH, SB_WIDTH, SB_WIDTH, HGRN_WIDTH, HGRN_WIDTH, HGRN_WIDTH, HGRN_WIDTH, D_MODEL, D_MODEL)
IN_WIDTH = sum(IN_SPLITS)


def layer_norm(x, g, b):
    xf = x.astype(jnp.float32)
    mu = jnp.mean(xf, axis=-1, keepdims=True)
    var = jnp.mean(jnp.square(xf - mu), axis=-1, keepdims=True)
    return ((xf - mu) * lax.rsqrt(var + LN_EPS) * g + b).astype(x.dtype)

def stick_breaking_attention(q, k, v):
    T = q.shape[2]
    scale = SB_HEAD_DIM ** -0.5
    qf, kf, vf = q.astype(jnp.float32), k.astype(jnp.float32), v.astype(jnp.float32)
    outs = []
    for blk in range(T // SB_BLOCK):
        t0 = blk * SB_BLOCK
        t1 = t0 + SB_BLOCK
        z = jnp.einsum('bhtd,bhsd->bhts', qf[:, :, t0:t1], kf[:, :, :t1]) * scale
        mask = jnp.arange(t1)[None, :] < (t0 + jnp.arange(SB_BLOCK))[:, None]
        log_keep = jnp.where(mask, jax.nn.log_sigmoid(-z), 0.0)
        log_after = lax.cumsum(log_keep, axis=3, reverse=True) - log_keep
        weights = jnp.where(mask, jnp.exp(jax.nn.log_sigmoid(z) + log_after), 0.0)
        outs.append(jnp.einsum('bhts,bhsd->bhtd', weights, vf[:, :, :t1]))
    return jnp.concatenate(outs, axis=2).astype(q.dtype)

def hgrn2_recurrence(q, k, logf, v):
    B, T, H, dk = q.shape
    dv = v.shape[-1]
    n_chunks = T // HGRN_CHUNK

    def to_chunks(a):
        return a.reshape(B, n_chunks, HGRN_CHUNK, H, a.shape[-1]).transpose(1, 0, 3, 2, 4)

    causal = jnp.tril(jnp.ones((HGRN_CHUNK, HGRN_CHUNK), dtype=bool))

    def step(S, xs):
        qc, kc, gc, vc = xs
        b = jnp.cumsum(gc, axis=2)
        o_inter = jnp.einsum('bhtk,bhkv->bhtv', qc * jnp.exp(b), S)
        diff = b[:, :, :, None, :] - b[:, :, None, :, :]
        decay = jnp.exp(jnp.where(causal[:, :, None], diff, -jnp.inf))
        scores = jnp.einsum('bhtsk,bhsk->bhts', qc[:, :, :, None, :] * decay, kc)
        o = o_inter + jnp.einsum('bhts,bhsv->bhtv', scores, vc)
        b_last = b[:, :, -1:, :]
        S_new = jnp.exp(b_last[:, :, 0, :])[..., None] * S + jnp.einsum(
            'bhsk,bhsv->bhkv', kc * jnp.exp(b_last - b), vc)
        return S_new, o

    S0 = jnp.zeros((B, H, dk, dv), jnp.float32)
    _, o = lax.scan(step, S0, (to_chunks(q), to_chunks(k), to_chunks(logf), to_chunks(v)))
    return o.transpose(1, 0, 3, 2, 4).reshape(B, T, H, dv)

def hybrid_mixer(x, w_in, lower_bound, hgrn_norm_g, w_branch_sb, w_branch_hgrn, w_out):
    B, T, _ = x.shape
    proj = x @ w_in
    offsets = np.cumsum(IN_SPLITS)[:-1].tolist()
    sq, sk, sv, hq, hf, hi, hg, gate_sb, gate_hg = jnp.split(proj, offsets, axis=-1)

    def heads(a):
        return a.reshape(B, T, SB_HEADS, SB_HEAD_DIM).transpose(0, 2, 1, 3)
    o_sb = stick_breaking_attention(heads(sq), heads(sk), heads(sv))
    o_sb = o_sb.transpose(0, 2, 1, 3).reshape(B, T, SB_WIDTH)

    f = lower_bound + (1.0 - lower_bound) * jax.nn.sigmoid(hf.astype(jnp.float32))
    shp = (B, T, HGRN_HEADS, HGRN_HEAD_DIM)
    o_hg = hgrn2_recurrence(jax.nn.silu(hq.astype(jnp.float32)).reshape(shp),
                            (1.0 - f).reshape(shp),
                            jnp.log(f).reshape(shp),
                            hi.astype(jnp.float32).reshape(shp))
    o_hg = o_hg * lax.rsqrt(jnp.mean(jnp.square(o_hg), axis=-1, keepdims=True) + RMS_EPS)
    o_hg = (o_hg.reshape(B, T, HGRN_WIDTH) * hgrn_norm_g * jax.nn.sigmoid(hg.astype(jnp.float32))).astype(x.dtype)

    merged = jax.nn.sigmoid(gate_sb) * (o_sb @ w_branch_sb) + jax.nn.sigmoid(gate_hg) * (o_hg @ w_branch_hgrn)
    return merged @ w_out

def moe(h, router_w, router_b, w_up, b_up, w_down, b_down):
    B, T, D = h.shape
    N = B * T
    xt = h.reshape(N, D)
    logits = (xt @ router_w + router_b).astype(jnp.float32)
    top_vals, top_idx = lax.top_k(logits, TOP_K)
    gates = jax.nn.softmax(top_vals, axis=-1)

    e_flat = top_idx.reshape(-1)
    tok_flat = jnp.arange(N * TOP_K, dtype=jnp.int32) // TOP_K
    order = jnp.argsort(e_flat)
    e_sorted = e_flat[order]
    tok_sorted = tok_flat[order]
    gate_sorted = gates.reshape(-1)[order].astype(h.dtype)

    counts = jnp.bincount(e_flat, length=N_EXPERTS)
    padded = (counts + EXPERT_BLOCK - 1) // EXPERT_BLOCK * EXPERT_BLOCK
    start = jnp.cumsum(counts) - counts
    pad_end = jnp.cumsum(padded)
    pad_start = pad_end - padded
    dest = pad_start[e_sorted] + (jnp.arange(N * TOP_K) - start[e_sorted])

    cap = N * TOP_K + N_EXPERTS * (EXPERT_BLOCK - 1)
    n_blocks = -(-cap // EXPERT_BLOCK)
    n_slots = n_blocks * EXPERT_BLOCK
    slot_tok = jnp.full((n_slots,), N, dtype=jnp.int32).at[dest].set(tok_sorted)
    x_pad = jnp.concatenate([xt, jnp.zeros((1, D), xt.dtype)], axis=0)
    xb = x_pad[slot_tok].reshape(n_blocks, EXPERT_BLOCK, D)
    block_e = jnp.minimum(jnp.searchsorted(pad_end, jnp.arange(n_blocks) * EXPERT_BLOCK, side='right'),
                          N_EXPERTS - 1)

    def expert_block(args):
        xblk, e = args
        hcat = xblk @ w_up[e] + b_up[e]
        x_glu = jnp.minimum(hcat[:, 0::2], SWIGLU_LIMIT)
        x_lin = jnp.clip(hcat[:, 1::2], -SWIGLU_LIMIT, SWIGLU_LIMIT)
        act = x_glu * jax.nn.sigmoid(SWIGLU_ALPHA * x_glu) * (x_lin + 1.0)
        return act @ w_down[e] + b_down[e]

    y_slots = lax.map(expert_block, (xb, block_e)).reshape(n_slots, D)
    contrib = y_slots[dest] * gate_sorted[:, None]
    out = jax.ops.segment_sum(contrib, tok_sorted, num_segments=N)
    return out.reshape(B, T, D).astype(h.dtype)

def first_inputs(seed: int = 0) -> dict:
    key = jax.random.key(seed)
    ks = jax.random.split(key, 18)
    nrm = jax.random.normal
    beta = DEEPNORM_BETA
    col_scale = jnp.concatenate([jnp.full((w,), s, jnp.float32) for w, s in
                                 zip(IN_SPLITS, (1.0, 1.0, beta, 1.0, 1.0, beta, 1.0, 1.0, 1.0))])
    x = nrm(ks[0], (BATCH, SEQ, D_MODEL), jnp.float32)
    w_in = nrm(ks[1], (DEPTH, D_MODEL, IN_WIDTH), jnp.float32) * D_MODEL ** -0.5 * col_scale
    hgrn_lb_logits = 1.0 + 0.1 * nrm(ks[2], (DEPTH + 1, HGRN_WIDTH), jnp.float32)
    hgrn_norm_g = 1.0 + 0.05 * nrm(ks[3], (DEPTH, HGRN_WIDTH), jnp.float32)
    w_branch_sb = nrm(ks[4], (DEPTH, SB_WIDTH, D_MODEL), jnp.float32) * SB_WIDTH ** -0.5
    w_branch_hgrn = nrm(ks[5], (DEPTH, HGRN_WIDTH, D_MODEL), jnp.float32) * HGRN_WIDTH ** -0.5
    w_out = nrm(ks[6], (DEPTH, D_MODEL, D_MODEL), jnp.float32) * D_MODEL ** -0.5 * beta
    ln1_g = 1.0 + 0.05 * nrm(ks[7], (DEPTH, D_MODEL), jnp.float32)
    ln1_b = 0.02 * nrm(ks[8], (DEPTH, D_MODEL), jnp.float32)
    router_w = nrm(ks[9], (DEPTH, D_MODEL, N_EXPERTS), jnp.float32) * D_MODEL ** -0.5
    router_b = 0.01 * nrm(ks[10], (DEPTH, N_EXPERTS), jnp.float32)
    expert_w_up = nrm(ks[11], (DEPTH, N_EXPERTS, D_MODEL, 2 * D_FF), jnp.float32) * D_MODEL ** -0.5 * beta
    expert_b_up = 0.01 * nrm(ks[12], (DEPTH, N_EXPERTS, 2 * D_FF), jnp.float32)
    expert_w_down = nrm(ks[13], (DEPTH, N_EXPERTS, D_FF, D_MODEL), jnp.float32) * D_FF ** -0.5 * beta
    expert_b_down = 0.01 * nrm(ks[14], (DEPTH, N_EXPERTS, D_MODEL), jnp.float32)
    ln2_g = 1.0 + 0.05 * nrm(ks[15], (DEPTH, D_MODEL), jnp.float32)
    ln2_b = 0.02 * nrm(ks[16], (DEPTH, D_MODEL), jnp.float32)
    return {'x': x, 'w_in': w_in, 'hgrn_lb_logits': hgrn_lb_logits, 'hgrn_norm_g': hgrn_norm_g,
            'w_branch_sb': w_branch_sb, 'w_branch_hgrn': w_branch_hgrn, 'w_out': w_out,
            'ln1_g': ln1_g, 'ln1_b': ln1_b, 'router_w': router_w, 'router_b': router_b,
            'expert_w_up': expert_w_up, 'expert_b_up': expert_b_up,
            'expert_w_down': expert_w_down, 'expert_b_down': expert_b_down,
            'ln2_g': ln2_g, 'ln2_b': ln2_b}

def first_block(x, w_in, hgrn_lb_logits, hgrn_norm_g, w_branch_sb, w_branch_hgrn, w_out,
              ln1_g, ln1_b, router_w, router_b, expert_w_up, expert_b_up,
              expert_w_down, expert_b_down, ln2_g, ln2_b):
    lower_bounds = jnp.cumsum(jax.nn.softmax(hgrn_lb_logits.astype(jnp.float32), axis=0), axis=0)
    h = x
    for l in range(DEPTH):
        mix = hybrid_mixer(h, w_in[l], lower_bounds[l], hgrn_norm_g[l],
                           w_branch_sb[l], w_branch_hgrn[l], w_out[l])
        h = layer_norm(DEEPNORM_ALPHA * h + mix, ln1_g[l], ln1_b[l])
        ffn = moe(h, router_w[l], router_b[l], expert_w_up[l], expert_b_up[l],
                  expert_w_down[l], expert_b_down[l])
        h = layer_norm(DEEPNORM_ALPHA * h + ffn, ln2_g[l], ln2_b[l])
    return h


D_CONV = D_MODEL
CONV_A_WIDTH = 3
EXPAND = 2
D_INNER = EXPAND * D_MODEL
HEAD_DIM = 64
N_HEADS = D_INNER // HEAD_DIM
N_GROUPS = 4
D_STATE = 128
SSD_CONV_WIDTH = 4
CHUNK = 128
D_XBC = D_INNER + 2 * N_GROUPS * D_STATE
D_FF_2 = 2816
FFN_CONV_WIDTH = 3
N_IN = 2 * D_MODEL + 3 * D_CONV + D_INNER + D_XBC + N_HEADS
EPS = 1e-5
DT_MIN = 1e-3
DT_MAX = 1e-1


def rmsnorm(x, w):
    xf = x.astype(jnp.float32)
    y = xf * lax.rsqrt(jnp.mean(xf * xf, axis=-1, keepdims=True) + EPS)
    return (y * w.astype(jnp.float32)).astype(x.dtype)

def causal_dwconv(x, w):
    k, c = w.shape
    return lax.conv_general_dilated(
        x, w[:, None, :].astype(x.dtype), window_strides=(1,), padding=[(k - 1, 0)],
        dimension_numbers=("NWC", "WIO", "NWC"), feature_group_count=c)

def ssd_chunked_scan(xh, dt, a, bmat, cmat):
    b, s, h, p = xh.shape
    g, n = bmat.shape[-2:]
    j = h // g
    c = s // CHUNK
    x_ = (xh.astype(jnp.float32) * dt[..., None]).reshape(b, c, CHUNK, g, j, p)
    log_a = jnp.moveaxis((dt * a).reshape(b, c, CHUNK, g, j), 2, -1)
    bc = bmat.astype(jnp.float32).reshape(b, c, CHUNK, g, n)
    cc = cmat.astype(jnp.float32).reshape(b, c, CHUNK, g, n)
    a_cum = jnp.cumsum(log_a, axis=-1)

    causal = jnp.tril(jnp.ones((CHUNK, CHUNK), dtype=bool))
    seg = a_cum[..., :, None] - a_cum[..., None, :]
    decay_in = jnp.exp(jnp.where(causal, seg, -jnp.inf))
    cb = jnp.einsum("bclgn,bcsgn->bcgls", cc, bc)
    y_diag = jnp.einsum("bcgjls,bcsgjp->bclgjp", cb[:, :, :, None] * decay_in, x_)

    decay_to_end = jnp.exp(a_cum[..., -1:] - a_cum)
    states = jnp.einsum("bclgn,bcgjl,bclgjp->bcgjpn", bc, decay_to_end, x_)
    chunk_decay = jnp.exp(a_cum[..., -1])

    def step(carry, inp):
        st, dec = inp
        return carry * dec[..., None, None] + st, carry

    init = jnp.zeros((b, g, j, p, n), jnp.float32)
    _, prev = lax.scan(step, init, (jnp.moveaxis(states, 1, 0), jnp.moveaxis(chunk_decay, 1, 0)))
    prev = jnp.moveaxis(prev, 0, 1)
    y_off = jnp.einsum("bclgn,bcgjpn,bcgjl->bclgjp", cc, prev, jnp.exp(a_cum))
    return (y_diag + y_off).reshape(b, s, h, p)

def gated_group_rmsnorm(y, z, w):
    bsz, s, d = y.shape
    yf = (y.astype(jnp.float32) * jax.nn.silu(z.astype(jnp.float32))).reshape(bsz, s, N_GROUPS, d // N_GROUPS)
    yf = yf * lax.rsqrt(jnp.mean(yf * yf, axis=-1, keepdims=True) + EPS)
    return (yf.reshape(bsz, s, d) * w.astype(jnp.float32)).astype(y.dtype)

def hybrid_mixer_2(u, w_in, conv_a_w, w_a_out, ssd_conv_w, ssd_conv_b, dt_bias, a_log,
                 d_skip, ssd_norm_w, w_s_out, w_o):
    bsz, s, _ = u.shape
    proj = u @ w_in
    sizes = [D_MODEL, D_MODEL, D_CONV, D_CONV, D_CONV, D_INNER, D_XBC, N_HEADS]
    offsets = np.cumsum(sizes)[:-1].tolist()
    gate_a, gate_s, b_a, c_a, v_a, z, xbc, dt_raw = jnp.split(proj, offsets, axis=-1)

    y_a = (b_a * causal_dwconv(c_a * v_a, conv_a_w)) @ w_a_out

    xbc = jax.nn.silu(causal_dwconv(xbc, ssd_conv_w) + ssd_conv_b)
    xs, bs, cs = jnp.split(xbc, [D_INNER, D_INNER + N_GROUPS * D_STATE], axis=-1)
    xh = xs.reshape(bsz, s, N_HEADS, HEAD_DIM)
    dt = jax.nn.softplus(dt_raw.astype(jnp.float32) + dt_bias.astype(jnp.float32))
    a = -jnp.exp(a_log.astype(jnp.float32))
    y = ssd_chunked_scan(xh, dt, a,
                         bs.reshape(bsz, s, N_GROUPS, D_STATE),
                         cs.reshape(bsz, s, N_GROUPS, D_STATE))
    y = y + d_skip.astype(jnp.float32)[:, None] * xh.astype(jnp.float32)
    y = y.reshape(bsz, s, D_INNER).astype(u.dtype)
    y_s = gated_group_rmsnorm(y, z, ssd_norm_w) @ w_s_out

    merged = jax.nn.sigmoid(gate_a) * y_a + jax.nn.sigmoid(gate_s) * y_s
    return merged @ w_o

def conv_gated_mlp(v, w_up, ffn_conv_w, ffn_conv_b, w_down):
    hv = v @ w_up
    h1, h3 = jnp.split(hv, 2, axis=-1)
    h1 = causal_dwconv(h1, ffn_conv_w) + ffn_conv_b
    return (jax.nn.silu(h1) * h3) @ w_down

def second_inputs(seed: int = 0) -> dict:
    key = jax.random.key(seed)
    ks = jax.random.split(key, 24)
    f32 = jnp.float32

    def nrm(k, shape, scale):
        return jax.random.normal(k, shape, f32) * scale

    dt0 = jnp.exp(jax.random.uniform(ks[9], (DEPTH, N_HEADS), f32)
                  * (np.log(DT_MAX) - np.log(DT_MIN)) + np.log(DT_MIN))
    dt_bias = dt0 + jnp.log(-jnp.expm1(-dt0))
    return {
        "x": nrm(ks[0], (BATCH, SEQ, D_MODEL), 1.0),
        "norm_mix_w": 1.0 + nrm(ks[1], (DEPTH, D_MODEL), 0.02),
        "w_in": nrm(ks[2], (DEPTH, D_MODEL, N_IN), D_MODEL ** -0.5),
        "conv_a_w": nrm(ks[3], (DEPTH, CONV_A_WIDTH, D_CONV), CONV_A_WIDTH ** -0.5),
        "w_a_out": nrm(ks[4], (DEPTH, D_CONV, D_MODEL), D_CONV ** -0.5),
        "ssd_conv_w": nrm(ks[5], (DEPTH, SSD_CONV_WIDTH, D_XBC), SSD_CONV_WIDTH ** -0.5),
        "ssd_conv_b": nrm(ks[6], (DEPTH, D_XBC), 0.02),
        "dt_bias": dt_bias,
        "a_log": jnp.log(jax.random.uniform(ks[7], (DEPTH, N_HEADS), f32, 1.0, 16.0)),
        "d_skip": 1.0 + nrm(ks[8], (DEPTH, N_HEADS), 0.02),
        "ssd_norm_w": 1.0 + nrm(ks[10], (DEPTH, D_INNER), 0.02),
        "w_s_out": nrm(ks[11], (DEPTH, D_INNER, D_MODEL), D_INNER ** -0.5),
        "w_o": nrm(ks[12], (DEPTH, D_MODEL, D_MODEL), D_MODEL ** -0.5),
        "norm_ffn_w": 1.0 + nrm(ks[13], (DEPTH, D_MODEL), 0.02),
        "w_up": nrm(ks[14], (DEPTH, D_MODEL, 2 * D_FF_2), D_MODEL ** -0.5),
        "ffn_conv_w": nrm(ks[15], (DEPTH, FFN_CONV_WIDTH, D_FF_2), FFN_CONV_WIDTH ** -0.5),
        "ffn_conv_b": nrm(ks[16], (DEPTH, D_FF_2), 0.02),
        "w_down": nrm(ks[17], (DEPTH, D_FF_2, D_MODEL), D_FF_2 ** -0.5),
        "final_norm_w": 1.0 + nrm(ks[18], (D_MODEL,), 0.02),
    }

def second_block(x, norm_mix_w, w_in, conv_a_w, w_a_out, ssd_conv_w, ssd_conv_b, dt_bias,
              a_log, d_skip, ssd_norm_w, w_s_out, w_o, norm_ffn_w, w_up, ffn_conv_w,
              ffn_conv_b, w_down, final_norm_w):
    h = x
    for l in range(DEPTH):
        u = rmsnorm(h, norm_mix_w[l])
        h = h + hybrid_mixer_2(u, w_in[l], conv_a_w[l], w_a_out[l], ssd_conv_w[l], ssd_conv_b[l],
                             dt_bias[l], a_log[l], d_skip[l], ssd_norm_w[l], w_s_out[l], w_o[l])
        v = rmsnorm(h, norm_ffn_w[l])
        h = h + conv_gated_mlp(v, w_up[l], ffn_conv_w[l], ffn_conv_b[l], w_down[l])
    return rmsnorm(h, final_norm_w)


def setup_inputs(seed=0):
    out = dict(first_inputs(seed))
    for name, value in second_inputs(seed + 1).items():
        if name != "x":
            out[name + "_2"] = value
    return out


def reference(
    x, w_in, hgrn_lb_logits, hgrn_norm_g, w_branch_sb, w_branch_hgrn, w_out, ln1_g, ln1_b,
    router_w, router_b, expert_w_up, expert_b_up, expert_w_down, expert_b_down, ln2_g, ln2_b,
    norm_mix_w_2, w_in_2, conv_a_w_2, w_a_out_2, ssd_conv_w_2, ssd_conv_b_2, dt_bias_2, a_log_2,
    d_skip_2, ssd_norm_w_2, w_s_out_2, w_o_2, norm_ffn_w_2, w_up_2, ffn_conv_w_2, ffn_conv_b_2,
    w_down_2, final_norm_w_2,
):
    x = first_block(
        x, w_in, hgrn_lb_logits, hgrn_norm_g, w_branch_sb, w_branch_hgrn, w_out, ln1_g, ln1_b,
        router_w, router_b, expert_w_up, expert_b_up, expert_w_down, expert_b_down, ln2_g,
        ln2_b,
    )
    return second_block(
        x, norm_mix_w_2, w_in_2, conv_a_w_2, w_a_out_2, ssd_conv_w_2, ssd_conv_b_2, dt_bias_2,
        a_log_2, d_skip_2, ssd_norm_w_2, w_s_out_2, w_o_2, norm_ffn_w_2, w_up_2, ffn_conv_w_2,
        ffn_conv_b_2, w_down_2, final_norm_w_2,
    )


_drawn_inputs = setup_inputs


def setup_inputs(seed=0):
    import zlib

    import numpy as np

    out = dict(_drawn_inputs(seed))
    spreads = {}
    factors = {'hgrn_lb_logits': 8.0,
     'hgrn_norm_g': 4.742,
     'router_b': 4.801,
     'expert_b_up': 8.0,
     'expert_b_down': 8.0,
     'ssd_conv_b_2': 4.252,
     'd_skip_2': 8.0,
     'ssd_norm_w_2': 5.812,
     'norm_ffn_w_2': 4.445,
     'ffn_conv_b_2': 6.36,
     'final_norm_w_2': 2.781}
    for name, (base, spread) in spreads.items():
        noise = np.random.default_rng([zlib.crc32(name.encode()), seed]).standard_normal(out[name].shape)
        drawn = base * np.exp(spread * noise) if base else spread * noise
        out[name] = __import__('jax').numpy.asarray(drawn.astype(out[name].dtype))
    for name, factor in factors.items():
        out[name] = (out[name] * factor).astype(out[name].dtype)
    return out
```

```python
from contextlib import ExitStack

import numpy as np

import concourse.bass as bass
from concourse import mybir
from concourse.alu_op_type import AluOpType as ALU

FP32 = mybir.dt.float32
F32R = mybir.dt.float32r
INT32 = mybir.dt.int32
ACT = mybir.ActivationFunctionType
AX = mybir.AxisListType

P = 128
T = 256
TT = T // P
D = 1024
KD = D // P
COLS = 256
RING = 3

SB_HEADS, SB_DIM = 8, 64
HG_HEADS, HG_DIM = 4, 128
N_EXPERTS, TOP_K, SLOTS = 32, 4, 64
EXPERT_UNITS = 6
PASSES = T // SLOTS
DEEPNORM_ALPHA = 2.0 ** 0.25
LN_EPS, HG_EPS, RMS_EPS = 1e-5, 1e-6, 1e-5
NEG = -1.0e30
HALVES = [64, 32, 16, 8, 4, 2, 1]

SHARED = ["identity", "strict_upper", "causal", "strict_lower", "ones", "mean512", "stack_iota"]
MIXER1 = ["neg_tri", "neg_diag", "neg_ones", "mean128"] + [f"level{h}" for h in HALVES]


def shape_constants():
    a, b = np.arange(P)[:, None], np.arange(P)[None, :]
    c = {
        "identity": a == b,
        "strict_upper": a < b,
        "causal": a <= b,
        "strict_lower": a > b,
        "ones": np.ones((P, P)),
        "mean512": np.full((P, P), 1.0 / 512),
        "stack_iota": np.where(b < 64, a % 64 == b, b - 64.0),
        "neg_tri": -1.0 * (a >= b),
        "neg_diag": np.where(a < b, 0.0, NEG),
        "neg_ones": -np.ones((P, P)),
        "mean128": np.full((P, P), 1.0 / 128),
    }
    for h in HALVES:
        c[f"level{h}"] = (a // (2 * h) == b // (2 * h)) & (a % (2 * h) < h) & (b % (2 * h) >= h)
    return np.concatenate([np.asarray(c[n], np.float32) for n in SHARED + MIXER1], axis=1)


class Shared:
    pass


class Count:

    def __init__(self, eng, sem):
        self.eng, self.sem, self.n = eng, sem, 0

    def add(self, ins):
        ins.then_inc(self.sem, 1)
        self.n += 1
        return self.n

    def wait(self, n=None):
        self.eng.wait_ge(self.sem, self.n if n is None else n)


class Stream:

    def __init__(self, s, sem, name):
        self.s = s
        self.full = s.raw_full[name]
        self.hi_done = sem(f"{name}_hi_done")
        self.lo_done = sem(f"{name}_lo_done")
        self.gemm_done = sem(f"{name}_gemm_done")

    def load(self, sp, q, s, src, kt, cols):
        n = 3 * q + s
        if not (isinstance(q, int) and q == 0):
            sp.wait_ge(self.lo_done, n - 2)
        dst = self.s.raw[:, s, 0:kt * cols].rearrange("p (k n) -> p k n", k=kt)
        sp.dma_start(dst, src).then_inc(self.full[s], 16)

    def hi(self, act, q, s, size, gemms=None):
        act.wait_ge(self.full[s], 16 * (q + 1))
        if gemms is not None:
            act.wait_ge(self.gemm_done, gemms)
        act.activation(self.s.w_hi[:, s, 0:size], self.s.raw[:, s, 0:size], ACT.Copy).then_inc(self.hi_done, 1)

    def lo(self, dve, q, s, size):
        dve.wait_ge(self.hi_done, 3 * q + s + 1)
        dve.tensor_tensor(self.s.w_lo[:, s, 0:size], self.s.raw[:, s, 0:size],
                          self.s.w_hi[:, s, 0:size].bitcast(FP32), ALU.subtract).then_inc(self.lo_done, 1)

    def w(self, s, kt, cols):
        return (self.s.w_hi[:, s, 0:kt * cols].rearrange("p (k n) -> p k n", k=kt),
                self.s.w_lo[:, s, 0:kt * cols].rearrange("p (k n) -> p k n", k=kt))


def product3(pe, out, lhs, rhs, start, stop, shared=False):
    (ah, al), (bh, bl) = lhs, rhs
    pe.matmul(out, lhsT=ah, rhs=bh, start=start, stop=False, skip_group_check=shared)
    pe.matmul(out, lhsT=ah, rhs=bl, start=False, stop=False, skip_group_check=shared)
    return pe.matmul(out, lhsT=al, rhs=bh, start=False, stop=stop, skip_group_check=shared)


def features_out(pe, bank, w, x, j, kt, first=True, last=True):
    shared = not (first and last)
    for t in range(2):
        for k in range(kt):
            c = slice((2 * j + t) * P, (2 * j + t + 1) * P)
            m = product3(pe, bank[:, t * T:(t + 1) * T], (w[0][:, k, c], w[1][:, k, c]),
                         (x[0][:, k, :], x[1][:, k, :]), first and k == 0 and (t == 0 or not shared), last and k == kt - 1, shared)
    return m


def tokens_out(pe, bank, w, x, kt, x_of):
    for t in range(TT):
        for k in range(kt):
            c = slice(t * P, (t + 1) * P)
            m = product3(pe, bank[:, t * COLS:(t + 1) * COLS], (x_of(0, k)[:, c], x_of(1, k)[:, c]),
                         (w[0][:, k, :], w[1][:, k, :]), k == 0, k == kt - 1)
    return m


def layer_norm(dve, own, h, stats, mv, var_ready, rstd_ready, g, b, loaded, n_loaded, ready, per_tile=1):
    for t in range(TT):
        for c in range(2):
            own.add(dve.bn_stats(stats[:, t, c, :], h[:, t, 512 * c:512 * c + 512]))
        own.wait()
        dve.bn_aggr(mv[:, t, 0:2], stats[:, t, :, :].rearrange("p a c -> p (a c)")).then_inc(var_ready, 1)
    dve.wait_ge(loaded, n_loaded)
    for t in range(TT):
        dve.wait_ge(rstd_ready, per_tile * (t + 1))
        own.add(dve.tensor_scalar(h[:, t, :], h[:, t, :], mv[:, t, 0:1], mv[:, t, 3:4], op0=ALU.subtract, op1=ALU.mult))
        own.wait()
        own.add(dve.tensor_tensor(h[:, t, :], h[:, t, :], g, ALU.mult))
        own.wait()
        dve.tensor_tensor(h[:, t, :], h[:, t, :], b, ALU.add).then_inc(ready, 1)
    dve.wait_ge(ready, TT)


def mixer1(nc, A, s, out_dbg=None):
    with ExitStack() as ctx:
        def sb(name, shape, dt=FP32):
            return ctx.enter_context(nc.sbuf_tensor(name, shape, dt))

        sems = []

        def sem(name):
            sems.append(nc.alloc_semaphore(name))
            return sems[-1]

        sb_hi, sb_lo = sb("sb_hi", [P, 4, T], F32R), sb("sb_lo", [P, 4, T], F32R)
        hg_hi, hg_lo = sb("hg_hi", [P, 4, T], F32R), sb("hg_lo", [P, 4, T], F32R)
        x_hi, x_lo = sb("x_hi", [P, KD, T], F32R), sb("x_lo", [P, KD, T], F32R)
        s.w_hi = sb("m1_w_hi", [P, RING, KD * COLS], F32R)
        s.w_lo = sb("m1_w_lo", [P, RING, KD * COLS], F32R)
        con1 = sb("mixer1_constants", [P, len(MIXER1), P])
        early = s.expert_weights[:, :, :].rearrange("p u n -> p (u n)")

        def in_place(region, at, a, n):
            return region[:, at:at + a * n].rearrange("p (a n) -> p a n", a=a)

        scratch = early[:, 0:5632]
        v_tok = in_place(early, 5632, TT, 512)
        i_tok = in_place(early, 6656, TT, 512)
        hq, hk, hb, hlf = (in_place(early, 7680 + 1024 * i, HG_HEADS, T) for i in range(4))
        hg = sb("hgate", [P, HG_HEADS, T])
        half_g = sb("half_hgrn_norm", [P, HG_HEADS])
        gates = sb("gates", [P, 2 * KD, T])
        lb = sb("lower_bound", [P, 8, 4])
        stats, mv = sb("ln_stats", [P, TT, 2, 6]), sb("ln_mv", [P, TT, 4])
        rw, rb = sb("router_w", [P, KD, N_EXPERTS]), sb("router_b", [P, N_EXPERTS])
        lg = sb("logits", [P, TT, N_EXPERTS])
        rt = sb("route_tmp", [P, TT, 6, N_EXPERTS])
        top, cnt = sb("top8", [P, TT, 8]), sb("route_cols", [P, 16])

        def C(name):
            return s.con[:, SHARED.index(name), :] if name in SHARED else con1[:, MIXER1.index(name), :]

        q_t = scratch[:, 0:1024].rearrange("p (a t) -> p a t", a=4)
        k_t = scratch[:, 1024:2048].rearrange("p (a t) -> p a t", a=4)
        z = scratch[:, 2048:3584].rearrange("p (h b t) -> p h b t", h=4, b=3)
        z_flat = scratch[:, 2048:3584]
        spl = scratch[:, 3584:5120].rearrange("p (h b t) -> p h b t", h=4, b=3)
        spl_flat = scratch[:, 3584:5120]
        E = scratch[:, 0:1024]
        Q = scratch[:, 1024:2048]
        K = scratch[:, 2048:3072]
        tmp = scratch[:, 3072:4096]
        score = scratch[:, 4096:5632].rearrange("p (h b t) -> p h b t", h=4, b=3)

        def heads(ap):
            return ap.rearrange("p (h t) -> p h t", h=4)
        E4, Q4, K4, tmp4 = heads(E), heads(Q), heads(K), heads(tmp)
        flat = lambda t: t[:, :, :].rearrange("p h t -> p (h t)")
        q_f, k_f, b_f = flat(hq), flat(hk), flat(hb)
        hT = gates[:, 0:KD, :]
        ln_g, ln_b = (gates[:, 8 + 4 * i:12 + 4 * i, :].rearrange("p a t -> p (a t)") for i in range(2))

        st = Stream(s, sem, "m1")
        evacuated = [sem(f"m1_evacuated{i}") for i in range(2)]
        x_loaded, con_loaded, con1_loaded, small_loaded, ln_loaded = sem("x_loaded"), sem("con_loaded"), sem("con1_loaded"), sem("small_loaded"), sem("ln_loaded")
        rows_zero, rows_loaded, cols_ready = sem("rows_zero"), sem("rows_loaded"), sem("cols_ready")
        tr_done, tr_hi, tr_free = sem("tr_done"), sem("tr_hi"), sem("tr_free")
        act_own, dve_own = sem("m1_act_own"), sem("m1_dve_own")
        z_mm, z_out, sp_raw, sp_ready, tri_mm, w_sum, w_exp, pv_mm = (sem(n) for n in (
            "z_mm", "z_out", "sp_raw", "sp_ready", "tri_mm", "w_sum", "w_exp", "pv_mm"))
        sb_hi_done, sb_done = sem("sb_hi_done"), sem("sb_done")
        f_ready, lf_ready, q_tanh, e_args, e_ready, qk_ready, lv_mm, lv_tmp, lv_add, cross_out = (sem(n) for n in (
            "f_ready", "lf_ready", "q_tanh", "e_args", "e_ready", "qk_ready", "lv_mm", "lv_tmp", "lv_add", "cross_out"))
        o_mm, o_copy, o_square, ms_mm, rstd_ready, o_gated, hg_hi_done, hg_done = (sem(n) for n in (
            "o_mm", "o_copy", "o_square", "ms_mm", "rstd_ready", "o_gated", "hg_hi_done", "hg_done"))
        sbr_out, hgr_out, merged_hi, merged_done = (sem(n) for n in ("sbr_out", "hgr_out", "merged_hi", "merged_done"))
        bias_loaded, bias_mm, bias_ready = sem("bias_loaded"), sem("bias_mm"), sem("bias_ready")
        var_ready, ln_rstd, h_ready, ht_mm, ht_out, lg_mm = (sem(n) for n in (
            "var_ready", "ln_rstd", "h_ready", "ht_mm", "ht_out", "lg_mm"))
        top_ready, ex_ready, mask_ready, pos_mm, g_ready = (sem(n) for n in (
            "top_ready", "ex_ready", "mask_ready", "pos_mm", "g_ready"))

        SEG = {"sq": 0, "sk": 512, "sv": 1024, "hq": 1536, "hf": 2048, "hi": 2560, "hg": 3072, "gate": 3584}
        order = [(n, c) for n in ("sq", "sk", "sv", "hf", "hq", "hi", "hg") for c in (0, 1)]
        order += [("gate", c) for c in range(8)]
        NW = len(order)
        NB_UNITS, NO_UNITS = 4, 4
        bank_of_unit = list(range(NW)) + [NW + 2 * i for i in range(NB_UNITS)] + [NW + 8 + i for i in range(NO_UNITS)]
        gemms_after = [b + 1 for b in range(NW)] + [NW + 2 * i + 2 for i in range(NB_UNITS)] + [NW + 8 + i + 1 for i in range(NO_UNITS)]
        N_UNITS = NW + NB_UNITS + NO_UNITS

        def wait_bank(pe, b):
            if b >= 2:
                pe.wait_ge(evacuated[b % 2], b // 2)

        def split_hi(act, n):
            if n < N_UNITS:
                st.hi(act, n // 3, n % 3, KD * COLS, gemms_after[n - 3] if n >= 3 else None)

        def split_lo(dve, n):
            if n < N_UNITS:
                st.lo(dve, n // 3, n % 3, KD * COLS)

        with nc.Block() as block:
            @block.sync
            def _(sp):
                sp.dma_start(s.con[:, :, :], A["constants"][:, 0:len(SHARED) * P].rearrange("p (n c) -> p n c", c=P)).then_inc(con_loaded, 16)
                sp.dma_start(s.h[:, :, :], A["x"][0].rearrange("(a p) d -> p a d", p=P)).then_inc(x_loaded, 16)
                w_in = A["w_in"][0].rearrange("(k p) n -> p k n", p=P)
                for n, (seg, c) in enumerate(order):
                    c0 = SEG[seg] + COLS * c
                    st.load(sp, n // 3, n % 3, w_in[:, :, c0:c0 + COLS], KD, COLS)
                n = NW
                for name in ("w_branch_sb", "w_branch_hgrn"):
                    for c in range(2):
                        w = A[name][0].rearrange("(k p) n -> p k n", p=P)
                        st.load(sp, n // 3, n % 3, w[:, :, 512 * c:512 * c + 512], 4, 512)
                        n += 1
                for c in range(4):
                    w = A["w_out"][0].rearrange("(k p) n -> p k n", p=P)
                    st.load(sp, n // 3, n % 3, w[:, :, COLS * c:COLS * c + COLS], KD, COLS)
                    n += 1
                sp.wait_ge(hgr_out, 4)
                sp.dma_start(ln_g, A["ln1_g"][0].partition_broadcast(P)).then_inc(ln_loaded, 16)
                sp.dma_start(ln_b, A["ln1_b"][0].partition_broadcast(P)).then_inc(ln_loaded, 16)
                sp.wait_ge(hg_done, 4)
                for u in (1, 2, 3):
                    s.load_expert_unit(sp, u, 0)
                sp.wait_ge(st.gemm_done, NW + 8)
                s.load_expert_unit(sp, 4, 0)
                sp.wait_ge(st.lo_done, N_UNITS - 1)
                s.load_expert_unit(sp, 0, 0)
                sp.wait_ge(st.gemm_done, NW + 12)
                s.load_expert_unit(sp, 5, 0)

            @block.gpsimd
            def _(pool):
                pool.memset(s.rows[:, :, :], 0.0).then_inc(rows_zero, 1)
                pool.dma_start(con1[:, :, :], A["constants"][:, len(SHARED) * P:].rearrange("p (n c) -> p n c", c=P)).then_inc(con1_loaded, 16)
                pool.dma_start(s.dskip[0:16, :], A["d_skip_2"][0].rearrange("(j c) -> j c", c=2)).then_inc(small_loaded, 16)
                pool.dma_start(rw[:, :, :], A["router_w"][0].rearrange("(k p) n -> p k n", p=P)).then_inc(small_loaded, 16)
                pool.dma_start(rb[:, :], A["router_b"][0].partition_broadcast(P)).then_inc(small_loaded, 16)
                pool.wait_ge(rows_zero, 1)
                for name, (tile, r, n) in s.row_map.items():
                    src = A[name]
                    src = src[0] if name != "hgrn_lb_logits" else src
                    if len(src.shape) == 2:
                        src = src.rearrange("a (n c) -> (a n) c", c=P)
                    else:
                        src = src.rearrange("(n c) -> n c", c=P)
                    pool.dma_start(s.rows[r:r + n, tile, :], src).then_inc(rows_loaded, 16)
                b_up = A["expert_b_up"][0].rearrange("e (c n) -> (e c) n", n=256).rearrange("(r q) n -> q r n", q=P)
                pool.dma_start(s.bias_rows[:, :, :], b_up).then_inc(bias_loaded, 16)
                pool.dma_start(s.b_down[:, :], A["expert_b_down"][0]).then_inc(bias_loaded, 16)
                for j in range(1, 8):
                    pool.wait_ge(lv_tmp, 2 * (j + 1))
                    pool.tensor_tensor(score[:, :, 0:3:2, :], score[:, :, 0:3:2, :],
                                       tmp.rearrange("p (h b t) -> p h b t", h=4, b=2), ALU.add).then_inc(lv_add, 1)
                    pool.wait_ge(lv_add, j)

            @block.scalar
            def _(act):
                own = Count(act, act_own)
                for c in range(4):
                    act.wait_ge(tr_done, c + 1)
                    act.activation(x_hi[:, 2 * c:2 * c + 2, :].rearrange("p a t -> p (a t)"), s.bank[2 + c][:, :], ACT.Copy).then_inc(tr_hi, 1)
                for n in range(RING):
                    split_hi(act, n)

                def evac(n, dst, func, scale=1.0):
                    act.wait_ge(st.gemm_done, gemms_after[n])
                    act.activation(dst, s.bank[n % 2][:, :], func, scale=scale).then_inc(evacuated[n % 2], 1)
                    split_hi(act, n + 3)

                def pair(t, c):
                    return t[:, 2 * c:2 * c + 2, :].rearrange("p a t -> p (a t)")

                def z_copy(g):
                    for h in range(4):
                        act.wait_ge(z_mm, 4 * g + h + 1)
                        if g == 1 and h == 0:
                            act.wait_ge(pv_mm, 1)
                        act.activation(z[:, h, :, :].rearrange("p b t -> p (b t)"), s.bank[2 + h][:, 0:384], ACT.Copy).then_inc(z_out, 1)

                def softplus_parts(g):
                    act.wait_ge(z_out, 4 * g + 4)
                    if g == 1:
                        act.wait_ge(tri_mm, 4)
                    own.add(act.activation(spl_flat, z_flat, ACT.Abs))
                    own.wait()
                    own.add(act.activation(spl_flat, spl_flat, ACT.Exp, scale=-1.0))
                    own.wait()
                    act.activation(spl_flat, spl_flat, ACT.Ln, bias=1.0).then_inc(sp_raw, 1)

                def weights(g):
                    act.wait_ge(w_sum, 4 * g + 4)
                    act.activation(z_flat, z_flat, ACT.Exp).then_inc(w_exp, 1)

                def sb_out(g):
                    act.wait_ge(pv_mm, g + 1)
                    act.activation(pair(sb_hi, g), s.bank[6 + g][:, :], ACT.Copy).then_inc(sb_hi_done, 1)

                evac(0, pair(q_t, 0), ACT.Copy, SB_DIM ** -0.5)
                evac(1, pair(q_t, 1), ACT.Copy, SB_DIM ** -0.5)
                evac(2, pair(k_t, 0), ACT.Copy)
                evac(3, pair(k_t, 1), ACT.Copy)
                z_copy(0)
                softplus_parts(0)
                tok = lambda t, c: t[:, :, COLS * c:COLS * c + COLS]
                for c in range(2):
                    evac(4 + c, tok(v_tok, c), ACT.Copy)
                act.wait_ge(tr_done, 4 + 3)
                act.activation(s.cols[:, 0:3, :].rearrange("p a t -> p (a t)"), s.bank[6][:, 0:384], ACT.Copy).then_inc(cols_ready, 1)
                weights(0)
                act.wait_ge(cols_ready, 2)
                act.activation(lb[:, 2:4, :], lb[:, 0:2, :], ACT.Exp).then_inc(cols_ready, 1)
                for c in range(2):
                    evac(6 + c, pair(hk, c), ACT.Sigmoid)
                z_copy(1)
                softplus_parts(1)
                act.wait_ge(f_ready, 1)
                act.activation(flat(hlf), flat(hlf), ACT.Ln).then_inc(lf_ready, 1)
                for c in range(2):
                    act.wait_ge(st.gemm_done, 9 + c)
                    act.activation(pair(hq, c), s.bank[c][:, :], ACT.Tanh, scale=0.5).then_inc(q_tanh, 1)
                    split_hi(act, 11 + c)
                weights(1)
                for c in range(2):
                    evac(10 + c, tok(i_tok, c), ACT.Copy)
                sb_out(0)
                sb_out(1)
                for n in range(12, NW):
                    j = n - 12
                    if j < 8:
                        act.wait_ge(e_args, 2 * (j + 1))
                        act.activation(E, E, ACT.Exp).then_inc(e_ready, 1)
                    evac(n, pair(hg, n - 12) if n < 14 else pair(gates, n - 14), ACT.Tanh, 0.5)
                    if j == 1:
                        act.wait_ge(lv_mm, 1)
                        act.activation(score[:, :, 1, :], s.bank[2][:, :].rearrange("p (h t) -> p h t", h=4), ACT.Copy).then_inc(cross_out, 1)
                for c in range(2):
                    act.wait_ge(o_mm, c + 1)
                    act.activation(pair(Q4, c), s.bank[6 + c][:, :], ACT.Copy).then_inc(o_copy, 1)
                    act.activation(pair(K4, c), s.bank[6 + c][:, :], ACT.Square).then_inc(o_square, 1)
                for c in range(2):
                    act.wait_ge(ms_mm, c + 1)
                    own.add(act.activation(pair(E4, c), s.bank[2 + c][:, :], ACT.Ln, bias=s.eps_hg))
                own.wait()
                act.activation(E, E, ACT.Exp, scale=-0.5).then_inc(rstd_ready, 1)
                split_hi(act, NW + 3)
                act.wait_ge(o_gated, 1)
                for h in range(4):
                    act.activation(hg_hi[:, h, :], Q4[:, h, :], ACT.Copy, scale=half_g[:, h:h + 1]).then_inc(hg_hi_done, 1)
                act.wait_ge(bias_mm, 1)
                for r in range(2):
                    for kind in range(2):
                        j = 2 * r + kind
                        act.activation(s.bias_t[:, 16 * r:16 * r + 16, kind, :], s.bank[4][:, P * j:P * j + P].rearrange("p (e c) -> p e c", c=KD), ACT.Copy).then_inc(bias_ready, 1)
                split_hi(act, NW + 4)
                for c in range(4):
                    act.wait_ge(hgr_out, c + 1)
                    act.activation(pair(x_hi, c), pair(gates, c), ACT.Copy, scale=0.5).then_inc(merged_hi, 1)
                    if c == 1:
                        split_hi(act, NW + 5)
                split_hi(act, NW + 6)
                split_hi(act, NW + 7)
                for t in range(TT):
                    act.wait_ge(var_ready, t + 1)
                    own.add(act.activation(mv[:, t, 2:3], mv[:, t, 1:2], ACT.Ln, bias=s.eps_ln))
                    own.wait()
                    act.activation(mv[:, t, 3:4], mv[:, t, 2:3], ACT.Exp, scale=-0.5).then_inc(ln_rstd, 1)
                for c in range(4):
                    act.wait_ge(ht_mm, c + 1)
                    act.activation(hT[:, 4 * (c % 2):4 * (c % 2) + 4, P * (c // 2):P * (c // 2) + P],
                                   s.bank[2 + c][:, :].rearrange("p (k t) -> p k t", k=4), ACT.Copy).then_inc(ht_out, 1)
                act.wait_ge(top_ready, 2)
                for t in range(TT):
                    act.activation(rt[:, t, 0, :], lg[:, t, :], ACT.Exp, bias=cnt[:, t:t + 1]).then_inc(ex_ready, 1)

            @block.vector
            def _(dve):
                own = Count(dve, dve_own)
                step = own.add

                def sync_step(ins):
                    own.add(ins)
                    own.wait()

                step(dve.memset(s.eps[:, 0:1], LN_EPS))
                step(dve.memset(s.eps[:, 1:2], HG_EPS))
                step(dve.memset(s.slot[:, :, PASSES * N_EXPERTS:], -1.0))
                for c in range(4):
                    dve.wait_ge(tr_hi, c + 1)
                    sl = slice(2 * c, 2 * c + 2)
                    dve.tensor_tensor(x_lo[:, sl, :].rearrange("p a t -> p (a t)"), s.bank[2 + c][:, :],
                                      x_hi[:, sl, :].rearrange("p a t -> p (a t)").bitcast(FP32), ALU.subtract).then_inc(tr_free, 1)
                for n in range(RING):
                    split_lo(dve, n)
                diag = lambda name: C(name).unsqueeze(1).unsqueeze(1).to_broadcast([P, 4, 2, P])

                def softplus(g):
                    dve.wait_ge(sp_raw, g + 1)
                    sync_step(dve.scalar_tensor_tensor(out=spl_flat, in0=z_flat, scalar=0.0, in1=spl_flat, op0=ALU.max, op1=ALU.add))
                    dve.tensor_tensor(spl[:, :, 0:3:2, :], spl[:, :, 0:3:2, :], diag("strict_upper"), ALU.mult).then_inc(sp_ready, 1)
                    sync_step(dve.tensor_tensor(z[:, :, 0:3:2, :], z[:, :, 0:3:2, :], diag("neg_diag"), ALU.add))

                def exponents(g):
                    for h in range(4):
                        dve.wait_ge(tri_mm, 4 * g + h + 1)
                        zz = z[:, h, :, :].rearrange("p b t -> p (b t)")
                        dve.tensor_tensor(zz, s.bank[2 + h][:, 0:384], zz, ALU.add).then_inc(w_sum, 1)

                def low(dst, bank, hi, ready, signal):
                    dve.wait_ge(ready[0], ready[1])
                    dve.tensor_tensor(dst, bank, hi.bitcast(FP32), ALU.subtract).then_inc(signal, 1)

                def pair(t, c):
                    return t[:, 2 * c:2 * c + 2, :].rearrange("p a t -> p (a t)")

                for n in range(3, 7):
                    split_lo(dve, n)
                dve.wait_ge(small_loaded, 48)
                dve.wait_ge(rows_zero, 1)
                dve.tensor_copy(s.rows[0:16, 0, :].rearrange("p (a c) -> p a c", a=2),
                                s.dskip[0:16, :].unsqueeze(2).to_broadcast([16, 2, 64])).then_inc(rows_zero, 1)
                dve.wait_ge(con1_loaded, 16)
                softplus(0)
                split_lo(dve, 7)
                split_lo(dve, 8)
                exponents(0)
                dve.wait_ge(cols_ready, 1)
                l0, l1 = s.colrange("hgrn_lb_logits", 0, 4), s.colrange("hgrn_lb_logits", 4, 4)
                step(dve.tensor_scalar(half_g[:, :], s.colrange("hgrn_norm_g", 0, HG_HEADS), 0.5, None, op0=ALU.mult))
                sync_step(dve.tensor_tensor(lb[:, 4, :], l0, l1, ALU.max))
                step(dve.tensor_tensor(lb[:, 0, :], l0, lb[:, 4, :], ALU.subtract))
                own.wait()
                dve.tensor_tensor(lb[:, 1, :], l1, lb[:, 4, :], ALU.subtract).then_inc(cols_ready, 1)
                for n in range(9, 11):
                    split_lo(dve, n)
                dve.wait_ge(cols_ready, 3)
                sync_step(dve.tensor_tensor(lb[:, 5, :], lb[:, 2, :], lb[:, 3, :], ALU.add))
                sync_step(dve.reciprocal(lb[:, 6, :], lb[:, 5, :]))
                sync_step(dve.tensor_tensor(lb[:, 4, :], lb[:, 2, :], lb[:, 6, :], ALU.mult))
                sync_step(dve.tensor_scalar(lb[:, 7, :], lb[:, 4, :], -1.0, 1.0, op0=ALU.mult, op1=ALU.add))
                dve.wait_ge(evacuated[0], 4)
                dve.wait_ge(evacuated[1], 4)
                for h in range(4):
                    step(dve.tensor_scalar(hlf[:, h, :], hk[:, h, :], lb[:, 7, h:h + 1], lb[:, 4, h:h + 1], op0=ALU.mult, op1=ALU.add))
                own.wait()
                dve.tensor_scalar(k_f, flat(hlf), -0.5, 0.5, op0=ALU.mult, op1=ALU.add).then_inc(f_ready, 1)
                softplus(1)
                for c in range(2):
                    dve.wait_ge(q_tanh, c + 1)
                    dve.scalar_tensor_tensor(out=pair(hq, c), in0=pair(hq, c), scalar=1.0, in1=s.bank[c][:, :],
                                             op0=ALU.add, op1=ALU.mult).then_inc(evacuated[c], 1)
                    split_lo(dve, 11 + c)
                exponents(1)
                split_lo(dve, 13)
                dve.wait_ge(lf_ready, 1)
                for h in range(4):
                    for t in range(TT):
                        c = slice(t * P, (t + 1) * P)
                        step(dve.tensor_tensor_scan(hb[:, h, c], C("ones"), hlf[:, h, c], 0.0, op0=ALU.mult, op1=ALU.add))
                own.wait()
                split_lo(dve, 14)
                for g in range(2):
                    low(pair(sb_lo, g), s.bank[6 + g][:, :], pair(sb_hi, g), (sb_hi_done, g + 1), sb_done)
                dve.wait_ge(sb_done, 2)
                step(dve.memset(Q, 0.0))
                step(dve.memset(K, 0.0))

                def halves(ap, h):
                    v = ap.rearrange("p (n two h) -> p n two h", two=2, h=h)
                    return v[:, :, 0, :], v[:, :, 1, :]

                def exponent_args(j):
                    if j == 0:
                        last = hb[:, :, P - 1:P].to_broadcast([P, 4, P])
                        dve.tensor_tensor(E4[:, :, 0:P], last, hb[:, :, 0:P], ALU.subtract).then_inc(e_args, 1)
                        dve.tensor_copy(E4[:, :, P:T], hb[:, :, P:T]).then_inc(e_args, 1)
                    else:
                        h = HALVES[j - 1]
                        (b0, b1), (e0, e1) = halves(b_f, h), halves(E, h)
                        ref = b0[:, :, h - 1:h].to_broadcast([P, 512 // h, h])
                        dve.tensor_tensor(e0, ref, b0, ALU.subtract).then_inc(e_args, 1)
                        dve.tensor_tensor(e1, b1, ref, ALU.subtract).then_inc(e_args, 1)

                exponent_args(0)
                for j in range(10):
                    n = 12 + j
                    if j < 8:
                        dve.wait_ge(e_ready, j + 1)
                        own.wait()
                        if j:
                            dve.wait_ge(lv_mm, j)
                        if j == 0:
                            dve.wait_ge(evacuated[0], 5)
                            dve.wait_ge(evacuated[1], 5)
                            dve.tensor_tensor(Q4[:, :, P:T], hq[:, :, P:T], E4[:, :, P:T], ALU.mult).then_inc(qk_ready, 1)
                            dve.tensor_tensor(K4[:, :, 0:P], hk[:, :, 0:P], E4[:, :, 0:P], ALU.mult).then_inc(qk_ready, 1)
                        else:
                            h = HALVES[j - 1]
                            (e0, e1), (q1, k0) = halves(E, h), (halves(q_f, h)[1], halves(k_f, h)[0])
                            dve.tensor_tensor(halves(Q, h)[1], q1, e1, ALU.mult).then_inc(qk_ready, 1)
                            dve.tensor_tensor(halves(K, h)[0], k0, e0, ALU.mult).then_inc(qk_ready, 1)
                        dve.wait_ge(qk_ready, 2 * (j + 1))
                        if j < 7:
                            exponent_args(j + 1)
                    if 2 <= j:
                        m = j - 1
                        name = f"level{HALVES[m - 1]}" if m < 8 else "identity"
                        mask = C(name).unsqueeze(1).to_broadcast([P, 4, P])
                        dve.wait_ge(lv_mm, m + 1)
                        if m >= 3:
                            dve.wait_ge(lv_add, m - 2)
                        for c in range(2):
                            src = s.bank[(2 if m % 2 else 4) + c][:, :].rearrange("p (b t) -> p b t", b=4)
                            if m == 1:
                                for hh in range(2):
                                    ins = dve.tensor_tensor(score[:, 2 * c + hh, 0:3:2, :], src[:, 2 * hh:2 * hh + 2, :], mask[:, 0:2, :], ALU.mult)
                                    if hh:
                                        ins.then_inc(lv_tmp, 1)
                                    else:
                                        step(ins)
                            else:
                                dst = tmp[:, 512 * c:512 * c + 512].rearrange("p (b t) -> p b t", b=4)
                                dve.tensor_tensor(dst, src, mask, ALU.mult).then_inc(lv_tmp, 1)
                        dve.wait_ge(lv_tmp, 2 * m)
                    split_lo(dve, n + 3)
                def gated_product(c, g):
                    b = NW + c
                    dve.wait_ge(st.gemm_done, b + 1)
                    dve.scalar_tensor_tensor(out=g, in0=g, scalar=1.0, in1=s.bank[b % 2][:, :], op0=ALU.add, op1=ALU.mult).then_inc(evacuated[b % 2], 1)

                for c in range(2):
                    gated_product(c, pair(gates, c))
                dve.wait_ge(rstd_ready, 1)
                dve.wait_ge(o_square, 2)
                sync_step(dve.tensor_tensor(Q, Q, E, ALU.mult))
                dve.scalar_tensor_tensor(out=Q, in0=flat(hg), scalar=1.0, in1=Q, op0=ALU.add, op1=ALU.mult).then_inc(o_gated, 1)
                dve.wait_ge(o_gated, 1)
                for h in range(4):
                    dve.wait_ge(hg_hi_done, h + 1)
                    dve.scalar_tensor_tensor(out=hg_lo[:, h, :], in0=Q4[:, h, :], scalar=half_g[:, h:h + 1],
                                             in1=hg_hi[:, h, :].bitcast(FP32), op0=ALU.mult, op1=ALU.subtract).then_inc(hg_done, 1)
                split_lo(dve, NW + 3)
                for c in range(2, 4):
                    gated_product(c, pair(gates, c))
                split_lo(dve, NW + 4)
                for c in range(4):
                    b = NW + 4 + c
                    gated_product(4 + c, pair(gates, 4 + c))
                    dve.wait_ge(evacuated[b % 2], b // 2 + 1)
                    dve.tensor_tensor(pair(gates, c), pair(gates, c), pair(gates, 4 + c), ALU.add).then_inc(hgr_out, 1)
                    dve.wait_ge(merged_hi, c + 1)
                    dve.scalar_tensor_tensor(out=pair(x_lo, c), in0=pair(gates, c), scalar=0.5, in1=pair(x_hi, c).bitcast(FP32),
                                             op0=ALU.mult, op1=ALU.subtract).then_inc(merged_done, 1)
                for u in range(5, 8):
                    split_lo(dve, NW + u)
                for c in range(4):
                    b = NW + 8 + c
                    dve.wait_ge(st.gemm_done, b + 1)
                    dve.scalar_tensor_tensor(out=s.h[:, :, COLS * c:COLS * c + COLS], in0=s.h[:, :, COLS * c:COLS * c + COLS],
                                             scalar=DEEPNORM_ALPHA, in1=s.bank[b % 2][:, :].rearrange("p (a n) -> p a n", a=2),
                                             op0=ALU.mult, op1=ALU.add).then_inc(evacuated[b % 2], 1)
                dve.wait_ge(evacuated[0], (NW + 12) // 2)
                dve.wait_ge(evacuated[1], (NW + 12) // 2)
                layer_norm(dve, own, s.h, stats, mv, var_ready, ln_rstd, ln_g, ln_b, ln_loaded, 32, h_ready)
                dve.wait_ge(lg_mm, 1)
                for t in range(TT):
                    step(dve.tensor_tensor(lg[:, t, :], s.bank[6][:, 32 * t:32 * t + 32], rb[:, :], ALU.add))
                own.wait()
                for t in range(TT):
                    step(dve.max(top[:, t, :], lg[:, t, :]))
                own.wait()
                for t in range(TT):
                    dve.tensor_scalar(cnt[:, t:t + 1], top[:, t, 0:1], -1.0, None, op0=ALU.mult).then_inc(top_ready, 1)
                for t in range(TT):
                    thr = top[:, t, TOP_K - 1:TOP_K]
                    step(dve.tensor_scalar(rt[:, t, 1, :], lg[:, t, :], thr, None, op0=ALU.is_gt))
                    step(dve.tensor_scalar(rt[:, t, 2, :], lg[:, t, :], thr, None, op0=ALU.is_equal))
                own.wait()
                for t in range(TT):
                    step(dve.tensor_reduce(cnt[:, 2 + t:3 + t], rt[:, t, 1, :], AX.X, ALU.add))
                    step(dve.tensor_tensor_scan(rt[:, t, 3, :], C("ones")[:, 0:N_EXPERTS], rt[:, t, 2, :], 0.0, op0=ALU.mult, op1=ALU.add))
                own.wait()
                for t in range(TT):
                    step(dve.tensor_scalar(cnt[:, 4 + t:5 + t], cnt[:, 2 + t:3 + t], -1.0, float(TOP_K), op0=ALU.mult, op1=ALU.add))
                own.wait()
                for t in range(TT):
                    step(dve.tensor_scalar(rt[:, t, 3, :], rt[:, t, 3, :], cnt[:, 4 + t:5 + t], None, op0=ALU.is_le))
                own.wait()
                for t in range(TT):
                    step(dve.tensor_tensor(rt[:, t, 2, :], rt[:, t, 2, :], rt[:, t, 3, :], ALU.mult))
                own.wait()
                for t in range(TT):
                    dve.tensor_tensor(rt[:, t, 1, :], rt[:, t, 1, :], rt[:, t, 2, :], ALU.add).then_inc(mask_ready, 1)
                dve.wait_ge(mask_ready, 2)
                dve.wait_ge(ex_ready, 2)
                for t in range(TT):
                    step(dve.tensor_tensor(rt[:, t, 0, :], rt[:, t, 0, :], rt[:, t, 1, :], ALU.mult))
                own.wait()
                for t in range(TT):
                    step(dve.tensor_reduce(cnt[:, 6 + t:7 + t], rt[:, t, 0, :], AX.X, ALU.add))
                own.wait()
                step(dve.reciprocal(cnt[:, 8:10], cnt[:, 6:8]))
                own.wait()
                for t in range(TT):
                    dve.tensor_scalar(s.gate[:, t, :], rt[:, t, 0, :], cnt[:, 8 + t:9 + t], None, op0=ALU.mult).then_inc(g_ready, 1)
                dve.wait_ge(pos_mm, 1)
                for t in range(TT):
                    step(dve.tensor_scalar(rt[:, t, 4, :], s.bank[7][:, 32 * t:32 * t + 32], 1.0, None, op0=ALU.add))
                step(dve.tensor_reduce(cnt[:, 10:11], s.bank[7][:, 64:96], AX.X, ALU.max))
                own.wait()
                for t in range(TT):
                    step(dve.tensor_tensor(rt[:, t, 5, :], rt[:, t, 4, :], rt[:, t, 1, :], ALU.mult))
                for b in range(1, PASSES):
                    step(dve.tensor_scalar(cnt[:, 10 + b:11 + b], cnt[:, 10:11], float(SLOTS * b), float(N_EXPERTS), op0=ALU.is_gt, op1=ALU.mult))
                own.wait()
                for t in range(TT):
                    for b in range(PASSES):
                        step(dve.tensor_scalar(s.slot[:, t, N_EXPERTS * b:N_EXPERTS * b + N_EXPERTS], rt[:, t, 5, :], -1.0 - SLOTS * b, None, op0=ALU.add))
                step(dve.tensor_tensor(cnt[:, 14:15], cnt[:, 11:12], cnt[:, 12:13], ALU.add))
                own.wait()
                step(dve.tensor_tensor(cnt[:, 15:16], cnt[:, 14:15], cnt[:, 13:14], ALU.add))
                own.wait()
                step(dve.tensor_scalar(s.n_steps[0:1, 0:1], cnt[0:1, 15:16], float(N_EXPERTS), None, op0=ALU.add))
                own.wait()

            @block.tensor
            def _(pe):
                pe.wait_ge(con_loaded, 16)
                pe.wait_ge(x_loaded, 16)
                for c in range(4):
                    for i in range(4):
                        k, t = 2 * c + i // 2, i % 2
                        m = pe.transpose(s.bank[2 + c][:, P * i:P * i + P], s.h[:, t, k * P:k * P + P], C("identity"))
                    m.then_inc(tr_done, 1)
                pe.wait_ge(tr_free, 4)

                def gemm(n):
                    st_w = st.w(n % 3, KD, COLS)
                    pe.wait_ge(st.lo_done, n + 1)
                    wait_bank(pe, n)
                    if order[n][0] in ("sv", "hi"):
                        m = tokens_out(pe, s.bank[n % 2], st_w, None, KD, lambda part, k: (x_hi, x_lo)[part][:, k, :])
                    else:
                        m = features_out(pe, s.bank[n % 2], st_w, (x_hi, x_lo), 0, KD)
                    m.then_inc(st.gemm_done, 1)

                def z_products(g):
                    pe.wait_ge(evacuated[0], 2)
                    pe.wait_ge(evacuated[1], 2)
                    for hh in range(4):
                        h = 4 * g + hh
                        r = slice(64 * (h % 2), 64 * (h % 2) + 64)
                        if g:
                            pe.wait_ge(w_sum, hh + 1)
                        pe.matmul(s.bank[2 + hh][:, 0:256], lhsT=k_t[r, h // 2, 0:P], rhs=q_t[r, h // 2, :], start=True, stop=True)
                        pe.matmul(s.bank[2 + hh][:, 256:384], lhsT=k_t[r, h // 2, P:T], rhs=q_t[r, h // 2, P:T], start=True, stop=True).then_inc(z_mm, 1)

                def tri_products(g):
                    if g == 0:
                        pe.wait_ge(con1_loaded, 16)
                    pe.wait_ge(sp_ready, g + 1)
                    pe.wait_ge(z_out, 4 * g + 4)
                    for hh in range(4):
                        bank = s.bank[2 + hh]
                        pe.matmul(bank[:, 0:128], lhsT=C("neg_tri"), rhs=spl[:, hh, 0, :], start=True, stop=True)
                        pe.matmul(bank[:, 128:256], lhsT=C("neg_tri"), rhs=spl[:, hh, 1, :], start=True, stop=False)
                        pe.matmul(bank[:, 128:256], lhsT=C("neg_ones"), rhs=spl[:, hh, 2, :], start=False, stop=True)
                        pe.matmul(bank[:, 256:384], lhsT=C("neg_tri"), rhs=spl[:, hh, 2, :], start=True, stop=True).then_inc(tri_mm, 1)

                def pv(g):
                    pe.wait_ge(w_exp, g + 1)
                    if g == 0:
                        pe.wait_ge(cols_ready, 1)
                    pe.wait_ge(evacuated[0], 3)
                    pe.wait_ge(evacuated[1], 3)
                    for hh in range(4):
                        h = 4 * g + hh
                        r, c = slice(64 * (h % 2), 64 * (h % 2) + 64), T * (hh // 2)
                        v = v_tok[:, :, 64 * h:64 * h + 64]
                        w = z[:, hh, :, :].rearrange("p b t -> p (b t)")
                        pe.matmul(s.bank[6 + g][r, c:c + T], lhsT=v[:, 0, :], rhs=w[:, 0:256], start=True, stop=False)
                        m = pe.matmul(s.bank[6 + g][r, c + P:c + T], lhsT=v[:, 1, :], rhs=w[:, 256:384], start=False, stop=True)
                    m.then_inc(pv_mm, 1)

                for n in range(4):
                    gemm(n)
                z_products(0)
                gemm(4)
                gemm(5)
                pe.wait_ge(rows_loaded, 16 * len(s.row_map))
                pe.wait_ge(rows_zero, 2)
                for i in range(3):
                    pe.transpose(s.bank[6][:, P * i:P * i + P], s.rows[:, i, :], C("identity")).then_inc(tr_done, 1)
                tri_products(0)
                gemm(6)
                gemm(7)
                pv(0)
                z_products(1)
                gemm(8)
                gemm(9)
                tri_products(1)
                gemm(10)
                gemm(11)
                pv(1)

                def level(j):
                    if j == 8:
                        q, k = hq, hk
                    else:
                        pe.wait_ge(qk_ready, 2 * (j + 1))
                        q, k = Q4, K4
                    if j == 0:
                        pe.wait_ge(w_sum, 8)
                        for h in range(4):
                            m = pe.matmul(s.bank[2][:, P * h:P * h + P], lhsT=k[:, h, 0:P], rhs=q[:, h, P:T], start=True, stop=True)
                    else:
                        if j == 1:
                            pe.wait_ge(cross_out, 1)
                        if j >= 3:
                            pe.wait_ge(lv_tmp, 2 * (j - 2))
                        for h in range(4):
                            for t in range(TT):
                                c = slice(t * P, (t + 1) * P)
                                i = 2 * h + t
                                bank = s.bank[(2 if j % 2 else 4) + i // 4]
                                m = pe.matmul(bank[:, P * (i % 4):P * (i % 4) + P], lhsT=k[:, h, c], rhs=q[:, h, c], start=True, stop=True)
                    m.then_inc(lv_mm, 1)

                for n in range(12, NW):
                    gemm(n)
                    if n - 12 < 9:
                        level(n - 12)
                def branch(u, between=None):
                    n = NW + u
                    w = st.w(n % 3, 4, 512)
                    x = (sb_hi, sb_lo) if u < 2 else (hg_hi, hg_lo)
                    pe.wait_ge(st.lo_done, n + 1)
                    for j in range(2):
                        b = NW + 2 * u + j
                        wait_bank(pe, b)
                        features_out(pe, s.bank[b % 2], w, x, j, 4).then_inc(st.gemm_done, 1)
                        if between and j == 0:
                            between()

                pe.wait_ge(sb_done, 2)
                pe.wait_ge(lv_add, 7)
                for h in range(4):
                    bank, c = s.bank[6 + h // 2], T * (h % 2)
                    v = i_tok[:, :, P * h:P * h + P]
                    pe.matmul(bank[:, c:c + T], lhsT=v[:, 0, :], rhs=score[:, h, 0:2, :].rearrange("p b t -> p (b t)"), start=True, stop=False)
                    m = pe.matmul(bank[:, c + P:c + T], lhsT=v[:, 1, :], rhs=score[:, h, 2, :], start=False, stop=True)
                    if h % 2:
                        m.then_inc(o_mm, 1)

                def mean_squares():
                    for c in range(2):
                        pe.wait_ge(o_square, c + 1)
                        pe.matmul(s.bank[2 + c][:, :], lhsT=C("mean128"), rhs=K[:, 512 * c:512 * c + 512], start=True, stop=True).then_inc(ms_mm, 1)

                branch(0, mean_squares)
                branch(1)
                pe.wait_ge(bias_loaded, 32)
                for r in range(2):
                    for kind in range(2):
                        j = 2 * r + kind
                        m = pe.transpose(s.bank[4][:, P * j:P * j + P], s.bias_rows[:, r, kind:256:2], C("identity"))
                m.then_inc(bias_mm, 1)
                pe.wait_ge(hg_done, 4)
                branch(2)
                branch(3)
                def merged_part(part, k):
                    if part == 0:
                        pe.wait_ge(merged_done, k // 2 + 1)
                    return (x_hi, x_lo)[part][:, k, :]

                for u in range(NO_UNITS):
                    n, b = NW + NB_UNITS + u, NW + 8 + u
                    pe.wait_ge(st.lo_done, n + 1)
                    wait_bank(pe, b)
                    tokens_out(pe, s.bank[b % 2], st.w(n % 3, KD, COLS), None, KD, merged_part).then_inc(st.gemm_done, 1)
                pe.wait_ge(bias_ready, 4)
                for c in range(4):
                    t = c // 2
                    pe.wait_ge(h_ready, t + 1)
                    for i in range(4):
                        k = 4 * (c % 2) + i
                        m = pe.transpose(s.bank[2 + c][:, P * i:P * i + P], s.h[:, t, k * P:k * P + P], C("identity"))
                    m.then_inc(ht_mm, 1)
                for t in range(TT):
                    pe.wait_ge(ht_out, 2 * t + 2)
                    for k in range(KD):
                        m = pe.matmul(s.bank[6][:, 32 * t:32 * t + 32], lhsT=hT[:, k, t * P:t * P + P], rhs=rw[:, k, :], start=(k == 0), stop=(k == KD - 1))
                m.then_inc(lg_mm, 1)
                pe.wait_ge(mask_ready, 2)
                m0, m1 = rt[:, 0, 1, :], rt[:, 1, 1, :]
                pe.matmul(s.bank[7][:, 0:32], lhsT=C("strict_upper"), rhs=m0, start=True, stop=True)
                pe.matmul(s.bank[7][:, 32:64], lhsT=C("strict_upper"), rhs=m1, start=True, stop=False)
                pe.matmul(s.bank[7][:, 32:64], lhsT=C("ones"), rhs=m0, start=False, stop=True)
                pe.matmul(s.bank[7][:, 64:96], lhsT=C("ones"), rhs=m0, start=True, stop=False)
                pe.matmul(s.bank[7][:, 64:96], lhsT=C("ones"), rhs=m1, start=False, stop=True).then_inc(pos_mm, 1)
        nc.clear_and_free_semaphores(sems)
        nc.all_engine_barrier()


def experts(nc, A, s):
    UNITS = EXPERT_UNITS
    DVE_STEPS = 5 + 2 * 4
    with ExitStack() as ctx:
        def sb(name, shape, dt=FP32):
            return ctx.enter_context(nc.sbuf_tensor(name, shape, dt))

        sems = []

        def sem(name):
            sems.append(nc.alloc_semaphore(name))
            return sems[-1]

        sb("late_units_place", [P, 2, KD * 512])
        bias_t, b_down = s.bias_t, s.b_down
        weights, full, load = s.expert_units, s.expert_full, s.load_expert_unit
        xg = sb("x_gathered", [P, KD, SLOTS])
        ub = sb("tokens_major", [P, 2, 512])
        pre, sig = sb("pre_act", [P, 2, 2, 2, SLOTS]), sb("sigmoids", [P, 2, 2, SLOTS])
        act_t = sb("activations", [P, KD, SLOTS])
        onehot, scaled = sb("onehot", [P, TT, SLOTS]), sb("onehot_gated", [P, TT, 2, SLOTS])
        scatter = sb("scatter", [P, T])
        step_cols, bias_now = sb("step_cols", [P, 2, TT]), sb("bias_now", [P, 2, KD])
        gate_t = sb("gate_t", [N_EXPERTS, T])
        ln_gb = sb("ln2_params", [P, 2, D])
        stats, mv = sb("ln2_stats", [P, TT, 2, 6]), sb("ln2_mv", [P, TT, 4])

        (unit_mm, unit_out, scattered, turned, bank_t_read, glu_ready, sig_ready, act_ready, onehot_ready,
         gather_mm, gather_out, scatter_mm, scatter_out, bias_now_ready, dve_own) = (sem(n) for n in (
            "unit_mm", "unit_out", "scattered", "turned", "bank_t_read", "glu_ready", "sig_ready", "act_ready",
            "onehot_ready", "gather_mm", "gather_out", "scatter_mm", "scatter_out", "bias_now_ready", "m2_dve_own"))
        ln_loaded, gate_mm, sum_ready, ln_own, var_ready, ln_rstd, h_ready = (sem(n) for n in (
            "ln2_loaded", "gate_mm", "sum_ready", "ln_own", "m2_var_ready", "m2_ln_rstd", "m2_h_ready"))
        C = lambda name: s.con[:, SHARED.index(name), :]
        stack, iota = C("stack_iota")[:, 0:SLOTS], C("stack_iota")[:, SLOTS:P]
        U, TB, GB, ACC = (0, 1), 2, 3, 4

        def n_steps(eng):
            return eng.value_load(s.n_steps[0:1, 0:1], min_val=N_EXPERTS, max_val=PASSES * N_EXPERTS)

        with nc.Block() as block:
            @block.sync
            def _(sp):
                s.load_first(sp, "m3", 2)
                n = n_steps(sp)
                with sp.Fori(0, n - 1) as i:
                    for u in range(UNITS):
                        sp.wait_ge(unit_mm, i * UNITS + u + 1)
                        load(sp, u, (i + 1) % N_EXPERTS)
                sp.wait_ge(bank_t_read, n * 4)
                for i in range(2):
                    s.load_first(sp, "m3", i)

            @block.gpsimd
            def _(pool):
                pool.dma_start(ln_gb[:, 0, :], A["ln2_g"][0].partition_broadcast(P)).then_inc(ln_loaded, 16)
                pool.dma_start(ln_gb[:, 1, :], A["ln2_b"][0].partition_broadcast(P)).then_inc(ln_loaded, 16)

            @block.scalar
            def _(act):
                for t in range(TT):
                    act.wait_ge(gate_mm, t + 1)
                    act.activation(gate_t[:, P * t:P * t + P], s.bank[U[t]][0:N_EXPERTS, 0:P], ACT.Copy).then_inc(unit_out, 1)

                def gather_copy(i):
                    act.wait_ge(gather_mm, i + 1)
                    act.activation(xg[:, :, :].rearrange("p k n -> p (k n)"), s.bank[GB][:, :], ACT.Copy).then_inc(gather_out, 1)

                def scatter_copy(i):
                    act.wait_ge(scatter_mm, i + 1)
                    act.activation(scatter[:, :], s.bank[GB][:, 0:T], ACT.Copy).then_inc(scatter_out, 1)

                def unit_copy(i, j):
                    act.wait_ge(unit_mm, i * UNITS + j + 1)
                    if j < 2:
                        act.wait_ge(scattered, i * 2 + j + 1)
                    else:
                        act.wait_ge(turned, i * 4 + j - 1)
                    act.activation(ub[:, j % 2, :], s.bank[U[j % 2]][:, :], ACT.Copy).then_inc(unit_out, 1)

                def sigmoid(i, u):
                    act.wait_ge(glu_ready, i * 4 + u + 1)
                    act.activation(sig[:, u % 2, :, :], pre[:, u % 2, 0, :, :], ACT.Sigmoid, scale=1.702).then_inc(sig_ready, 1)

                gather_copy(0)
                scatter_copy(0)
                n = n_steps(act)
                with act.Fori(0, n) as i:
                    unit_copy(i, 0)
                    unit_copy(i, 1)
                    sigmoid(i, 0)
                    unit_copy(i, 2)
                    sigmoid(i, 1)
                    unit_copy(i, 3)
                    sigmoid(i, 2)
                    sigmoid(i, 3)
                    gather_copy(i + 1)
                    unit_copy(i, 4)
                    unit_copy(i, 5)
                    scatter_copy(i + 1)
                for t in range(TT):
                    act.wait_ge(var_ready, t + 1)
                    act.activation(mv[:, t, 2:3], mv[:, t, 1:2], ACT.Ln, bias=s.eps_ln).then_inc(ln_rstd, 1)
                    act.wait_ge(ln_rstd, 2 * t + 1)
                    act.activation(mv[:, t, 3:4], mv[:, t, 2:3], ACT.Exp, scale=-0.5).then_inc(ln_rstd, 1)

            @block.vector
            def _(dve):
                def one_hots(i, base):
                    own_i = lambda k: dve.wait_ge(dve_own, base + k)
                    dve.tensor_copy(step_cols[:, 0, :], s.slot[:, :, bass.ds(i, 1)].rearrange("p t o -> p (t o)")).then_inc(dve_own, 1)
                    dve.tensor_copy(step_cols[:, 1, :], s.gate[:, :, bass.ds(i % N_EXPERTS, 1)].rearrange("p t o -> p (t o)")).then_inc(dve_own, 1)
                    own_i(2)
                    for t in range(TT):
                        dve.tensor_scalar(onehot[:, t, :], iota, step_cols[:, 0, t:t + 1], None, op0=ALU.is_equal).then_inc(dve_own, 1)
                    for t in range(TT):
                        ins = dve.tensor_scalar(scaled[:, t, :, :], iota.unsqueeze(1).to_broadcast([P, 2, SLOTS]), step_cols[:, 0, t:t + 1],
                                                step_cols[:, 1, t:t + 1], op0=ALU.is_equal, op1=ALU.mult)
                        ins.then_inc(onehot_ready if t else dve_own, 1)

                def bias_copy(i):
                    return dve.tensor_copy(bias_now[:, :, :].rearrange("p a k -> p (a k)"),
                                           bias_t[:, bass.ds(i % N_EXPERTS, 1), :, :].rearrange("p o a k -> p (o a k)"))

                one_hots(0, 0)
                bias_copy(0).then_inc(bias_now_ready, 1)
                n = n_steps(dve)
                with dve.Fori(0, n) as i:
                    base = i * DVE_STEPS + 5
                    dve.wait_ge(scatter_out, i + 1)
                    one_hots(i + 1, base)
                    k = 5
                    for u in range(4):
                        dve.wait_ge(bias_now_ready, i + 1)
                        dve.wait_ge(turned, i * 4 + u + 1)
                        both = pre[:, u % 2, :, :, :]
                        dve.tensor_tensor(both, s.bank[TB][:, 0:256].rearrange("p (a c n) -> p a c n", a=2, c=2),
                                          bias_now[:, :, 2 * u:2 * u + 2].unsqueeze(3).to_broadcast([P, 2, 2, SLOTS]), ALU.add).then_inc(bank_t_read, 1)
                        dve.wait_ge(bank_t_read, i * 4 + u + 1)
                        dve.tensor_scalar(both, both, 7.0, None, op0=ALU.min).then_inc(glu_ready, 1)
                        dve.wait_ge(glu_ready, i * 4 + u + 1)
                        lin = pre[:, u % 2, 1, :, :]
                        dve.tensor_scalar(lin, lin, -7.0, None, op0=ALU.max).then_inc(dve_own, 1)
                        dve.wait_ge(sig_ready, i * 4 + u + 1)
                        g = sig[:, u % 2, :, :]
                        dve.tensor_tensor(g, g, pre[:, u % 2, 0, :, :], ALU.mult).then_inc(dve_own, 1)
                        k += 2
                        dve.wait_ge(dve_own, base + k)
                        dve.scalar_tensor_tensor(out=act_t[:, 2 * u:2 * u + 2, :], in0=lin, scalar=1.0, in1=g,
                                                 op0=ALU.add, op1=ALU.mult).then_inc(act_ready, 1)
                    bias_copy(i + 1).then_inc(bias_now_ready, 1)
                dve.wait_ge(scattered, n * 2 + 2)
                for t in range(TT):
                    for c in range(2):
                        hc = s.h[:, t, 512 * c:512 * c + 512]
                        dve.scalar_tensor_tensor(out=hc, in0=hc, scalar=DEEPNORM_ALPHA, in1=s.bank[ACC + 2 * t + c][:, :],
                                                 op0=ALU.mult, op1=ALU.add).then_inc(sum_ready, 1)
                dve.wait_ge(sum_ready, 4)
                layer_norm(dve, Count(dve, ln_own), s.h, stats, mv, var_ready, ln_rstd, ln_gb[:, 0, :], ln_gb[:, 1, :], ln_loaded, 32, h_ready, per_tile=2)

            @block.tensor
            def _(pe):
                for t in range(TT):
                    pe.transpose(s.bank[U[t]][0:N_EXPERTS, 0:P], s.gate[:, t, :], C("identity")).then_inc(gate_mm, 1)
                pe.wait_ge(unit_out, 2)
                for c in range(2):
                    for t in range(TT):
                        m = pe.matmul(s.bank[ACC + 2 * t + c][:, :], lhsT=gate_t[:, P * t:P * t + P], rhs=b_down[:, 512 * c:512 * c + 512], start=True, stop=True)
                    m.then_inc(scattered, 1)

                def gather(i):
                    pe.wait_ge(onehot_ready, i + 1)
                    for k in range(KD):
                        for t in range(TT):
                            m = pe.matmul(s.bank[GB][:, SLOTS * k:SLOTS * k + SLOTS], lhsT=s.h[:, t, P * k:P * k + P], rhs=onehot[:, t, :],
                                          start=(t == 0), stop=(t == 1))
                    m.then_inc(gather_mm, 1)

                def turn_scatter(i):
                    pe.wait_ge(gather_out, i + 1)
                    for t in range(TT):
                        m = pe.transpose(s.bank[GB][:, P * t:P * t + P], scaled[:, t, :, :].rearrange("p a n -> p (a n)"), C("identity"))
                    m.then_inc(scatter_mm, 1)

                def product(i, j, x):
                    pe.wait_ge(full[j], (i + 1) * 16)
                    pe.wait_ge(unit_out, i * UNITS + j + 1)
                    for k in range(KD):
                        half = slice(64 * (k % 2), 64 * (k % 2) + 64)
                        m = pe.matmul(s.bank[U[j % 2]][half, :], lhsT=x[:, k, :], rhs=weights[j][:, k, :], start=(k < 2), stop=(k >= KD - 2))
                    m.then_inc(unit_mm, 1)

                def turn(i, u):
                    pe.wait_ge(unit_out, i * UNITS + u + 3)
                    if u:
                        pe.wait_ge(bank_t_read, i * 4 + u)
                    for kind in range(2):
                        for c in range(2):
                            o = 128 * kind + 64 * c
                            m = pe.matmul(s.bank[TB][:, o:o + SLOTS], lhsT=ub[:, u % 2, 256 * c + kind:256 * c + 256:2], rhs=stack, start=True, stop=True)
                    m.then_inc(turned, 1)

                gather(0)
                turn_scatter(0)
                n = n_steps(pe)
                with pe.Fori(0, n) as i:
                    pe.wait_ge(gather_out, i + 1)
                    product(i, 0, xg)
                    product(i, 1, xg)
                    for u in range(2):
                        turn(i, u)
                        product(i, 2 + u, xg)
                    for u in range(2, 4):
                        turn(i, u)
                    pe.wait_ge(scatter_out, i + 1)
                    gather(i + 1)
                    pe.wait_ge(act_ready, i * 4 + 4)
                    product(i, 4, act_t)
                    product(i, 5, act_t)
                    for c in range(2):
                        pe.wait_ge(unit_out, i * UNITS + 7 + c)
                        for t in range(TT):
                            m = pe.matmul(s.bank[ACC + 2 * t + c][:, :], lhsT=scatter[:, P * t:P * t + P], rhs=ub[:, c, :],
                                          start=False, stop=True, skip_group_check=True)
                        m.then_inc(scattered, 1)
                    turn_scatter(i + 1)
        nc.clear_and_free_semaphores(sems)
        nc.all_engine_barrier()


def mixer2(nc, A, s):
    XBC_TAPS, A_TAPS, N_HEADS, N_GROUPS = 4, 3, 32, 4
    with ExitStack() as ctx:
        def sb(name, shape, dt=FP32):
            return ctx.enter_context(nc.sbuf_tensor(name, shape, dt))

        sems = []

        def sem(name):
            sems.append(nc.alloc_semaphore(name))
            return sems[-1]

        s.w_hi = sb("m3_w_hi", [P, RING, KD * COLS], F32R)
        s.w_lo = sb("m3_w_lo", [P, RING, KD * COLS], F32R)
        u_hi, u_lo = sb("u_hi", [P, KD, T], F32R), sb("u_lo", [P, KD, T], F32R)
        ya_hi, ya_lo = sb("ya_hi", [P, KD, T], F32R), sb("ya_lo", [P, KD, T], F32R)
        bcv = sb("b_c_v", [P, 24, T])
        xbc = sb("x_b_c", [P, 24, T])
        zt = sb("z", [P, 16, T])
        gates = sb("gates_2", [P, 16, T])
        x_tok = bcv[:, 8:24, :].rearrange("p a t -> p (a t)").rearrange("p (t f) -> p t f", t=TT)
        decay = bcv[:, 0:6, :].rearrange("p a t -> p (a t)").rearrange("p (r h b) -> p r h b", r=2, h=2)
        squares = [bcv[:, 6:8, :].rearrange("p a t -> p (a t)"), sb("squares", [P, 2 * T])[:, :]]
        cbm = xbc[:, 16:22, :].rearrange("p a t -> p (a t)").rearrange("p (g n) -> p g n", g=4)
        stats, mv = sb("rms_stats", [P, TT, 2, 6]), sb("rms_mv", [P, TT, 5])
        w_dt, dt_bias, a_col = sb("w_dt", [P, KD, N_HEADS]), sb("dt_bias", [P, N_HEADS]), sb("a_log", [P, N_HEADS])
        dt, loga = sb("dt", [P, TT, N_HEADS]), sb("log_a", [P, TT, N_HEADS])
        dt_tmp = sb("dt_tmp", [P, TT, N_HEADS])
        shift = sb("decay_shift", [P, 3, N_HEADS])
        acum_hi, acum_lo = sb("acum_hi", [N_HEADS, T], F32R), sb("acum_lo", [N_HEADS, T], F32R)
        pick = sb("pick_head", [N_HEADS, N_HEADS], F32R)
        rstd = sb("group_rstd", [P, T])
        half_w = sb("half_norm_w", [P, 16])

        C = lambda name: s.con[:, SHARED.index(name), :]
        diag = rstd
        diag = diag[:, :].rearrange("p (t c) -> p t c", t=TT)
        st = Stream(s, sem, "m3")
        evac_sem = [sem(f"m3_evac{i}") for i in range(4)]
        (par_loaded, var_ready, r_ready, diag_ready, ut_mm, ut_hi, ut_lo, dt_mm, dt_raw, dt_ready, acum_mm,
         shift_ready, act_own, dve_own, pool_own) = (sem("m3_" + n) for n in (
            "par_loaded", "var_ready", "r_ready", "diag_ready", "ut_mm", "ut_hi", "ut_lo", "dt_mm", "dt_raw", "dt_ready",
            "acum_mm", "shift_ready", "act_own", "dve_own", "pool_own"))
        tap_done, xbc_ready, cv_ready, conv_a, ya_ready, ya_hi_done, ya_done = (sem("m3_" + n) for n in (
            "tap_done", "xbc_ready", "cv_ready", "conv_a", "ya_ready", "ya_hi_done", "ya_done"))
        (cb_mm, cbm_ready, xt_mm, xtok_ready, row_mm, decay_ready, m_ready, y_mm, y_ready, z_tanh, gated, squared,
         ms_mm, rstd_ready, normed, y_hi, y_done) = (sem("m3_" + n) for n in (
            "cb_mm", "cbm_ready", "xt_mm", "xtok_ready", "row_mm", "decay_ready", "m_ready", "y_mm", "y_ready", "z_tanh",
            "gated", "squared", "ms_mm", "rstd_ready", "normed", "y_hi", "y_done"))
        merged, merged_hi, merged_done, gate_tanh, h_done = (sem("m3_" + n) for n in (
            "merged", "merged_hi", "merged_done", "gate_tanh", "h_done"))

        cols = [2048 + COLS * c for c in range(12)] + [7168 + COLS * c for c in range(12)] + [COLS * c for c in range(4)]
        W_IN = {n: c for n, c in zip(range(28), cols)}
        W_IN.update({32 + c: 5120 + COLS * c for c in range(8)})
        W_IN.update({40 + c: 1024 + COLS * c for c in range(4)})
        S_OUT = [(c, kh) for kh in range(2) for c in range(4)]
        N_UNITS = 56
        bank_seq = [(n, n % 3) for n in range(44)]
        bank_seq += [(48 + c, c) for c in range(4)] + [(52 + c, c % 3) for c in range(4)]
        bank_of, use_of = {}, {}
        seen = [0, 0, 0, 0]
        for n, b in bank_seq:
            bank_of[n], use_of[n] = b, seen[b]
            seen[b] += 1
        for n in range(44, 48):
            bank_of[n], use_of[n] = bank_of[n + 4], use_of[n + 4]

        def split_hi(act, n):
            if n < N_UNITS:
                st.hi(act, n // 3, n % 3, KD * COLS, n - 2 if n >= 3 else None)

        def split_lo(dve, n):
            if n < N_UNITS:
                st.lo(dve, n // 3, n % 3, KD * COLS)

        def pair(t, c):
            return t[:, 2 * c:2 * c + 2, :].rearrange("p a t -> p (a t)")

        with nc.Block() as block:
            @block.sync
            def _(sp):
                w_in = A["w_in_2"][0].rearrange("(k p) n -> p k n", p=P)

                def unit(n):
                    if n in W_IN:
                        return w_in[:, :, W_IN[n]:W_IN[n] + COLS]
                    if n < 32:
                        return A["w_a_out_2"][0].rearrange("(k p) n -> p k n", p=P)[:, :, COLS * (n - 28):COLS * (n - 27)]
                    if n < 52:
                        cb, kh = S_OUT[n - 44]
                        return A["w_s_out_2"][0].rearrange("(a k p) n -> a p k n", p=P, k=KD)[kh, :, :, COLS * cb:COLS * cb + COLS]
                    return A["w_o_2"][0].rearrange("(k p) n -> p k n", p=P)[:, :, COLS * (n - 52):COLS * (n - 51)]

                for n in range(3, N_UNITS):
                    st.load(sp, n // 3, n % 3, unit(n), KD, COLS)
                for i in (2, 0, 1):
                    sp.wait_ge(st.lo_done, N_UNITS - 2 + (i + 1) % 3)
                    s.load_first(sp, "m4", i)

            @block.gpsimd
            def _(pool):
                pool.dma_start(w_dt[:, :, :], A["w_in_2"][0].rearrange("(k p) n -> p k n", p=P)[:, :, 10240:10272]).then_inc(par_loaded, 16)
                pool.dma_start(dt_bias[:, :], A["dt_bias_2"][0].partition_broadcast(P)).then_inc(par_loaded, 16)
                pool.dma_start(a_col[:, :], A["a_log_2"][0].partition_broadcast(P)).then_inc(par_loaded, 16)
                pool.wait_ge(evac_sem[2], 4)
                pool.wait_ge(evac_sem[1], 4)
                pool.wait_ge(evac_sem[0], 4)
                for j in range(4):
                    c = pair(bcv, 4 + j)
                    pool.tensor_tensor(c, c, pair(bcv, 8 + j), ALU.mult).then_inc(cv_ready, 1)
                for j in range(4):
                    pool.wait_ge(conv_a, j + 1)
                    pool.wait_ge(cv_ready, 4)
                    pool.tensor_tensor(pair(bcv, j), pair(bcv, j), pair(bcv, 8 + j), ALU.mult).then_inc(ya_ready, 1)
                for g in range(N_GROUPS):
                    y = xbc[:, 4 * g:4 * g + 4, :].rearrange("p a t -> p (a t)")
                    pool.wait_ge(y_ready, 4 * g + 4)
                    pool.wait_ge(evac_sem[(33 + 2 * g) % 3], use_of[33 + 2 * g] + 1)
                    pool.wait_ge(evac_sem[(32 + 2 * g) % 3], use_of[32 + 2 * g] + 1)
                    pool.tensor_tensor(y, y, zt[:, 4 * g:4 * g + 4, :].rearrange("p a t -> p (a t)"), ALU.mult).then_inc(gated, 1)
                    pool.wait_ge(rstd_ready, g + 1)
                    pool.wait_ge(gated, g + 1)
                    pool.tensor_tensor(xbc[:, 4 * g:4 * g + 4, :], xbc[:, 4 * g:4 * g + 4, :],
                                       rstd[:, :].unsqueeze(1).to_broadcast([P, 4, T]), ALU.mult).then_inc(normed, 1)

            @block.scalar
            def _(act):
                own = Count(act, act_own)
                split_hi(act, 0)
                own.add(act.activation(pick[:, :], C("identity")[0:N_HEADS, 0:N_HEADS], ACT.Copy))
                for t in range(TT):
                    act.wait_ge(var_ready, t + 1)
                    own.add(act.activation(mv[:, t, 3:4], mv[:, t, 2:3], ACT.Ln, bias=s.eps_ln))
                    own.wait()
                    act.activation(mv[:, t, 4:5], mv[:, t, 3:4], ACT.Exp, scale=-0.5).then_inc(r_ready, 1)
                for k in range(KD):
                    act.wait_ge(ut_mm, k // 2 + 1)
                    act.activation(u_hi[:, k, :], s.bank[3 + k // 2][:, T * (k % 2):T * (k % 2) + T], ACT.Copy, scale=s.col("norm_mix_w_2", k)).then_inc(ut_hi, 1)
                    if k % 4 == 3:
                        split_hi(act, 1 + k // 4)
                act.wait_ge(dt_raw, 1)
                own.add(act.activation(dt_tmp[:, :, :], dt[:, :, :], ACT.Abs))
                own.wait()
                own.add(act.activation(dt_tmp[:, :, :], dt_tmp[:, :, :], ACT.Exp, scale=-1.0))
                act.wait_ge(par_loaded, 48)
                own.add(act.activation(a_col[:, :], a_col[:, :], ACT.Exp))
                own.wait()
                act.activation(dt_tmp[:, :, :], dt_tmp[:, :, :], ACT.Ln, bias=1.0).then_inc(dt_raw, 1)

                def evac(n, dst, func, scale=1.0, signal=None):
                    act.wait_ge(st.gemm_done, n + 1)
                    act.activation(dst, s.bank[bank_of[n]][:, :], func, scale=scale).then_inc(signal or evac_sem[bank_of[n]], 1)

                for n in range(12):
                    evac(n, pair(bcv, n), ACT.Copy)
                    split_hi(act, n + 3)

                def ya_part(j):
                    act.wait_ge(ya_ready, j + 1)
                    act.activation(pair(ya_hi, j), pair(bcv, j), ACT.Copy).then_inc(ya_hi_done, 1)

                for n in range(12, 24):
                    m = n - 12
                    act.wait_ge(st.gemm_done, n + 1)
                    for t in range(2):
                        act.activation(xbc[:, 2 * m + t, :], s.bank[n % 3][:, T * t:T * t + T], ACT.Identity,
                                       scale=s.col("ssd_conv_w_2", 24 * 3 + 2 * m + t), bias=s.col("ssd_conv_b_2", 2 * m + t)).then_inc(tap_done, 1)
                    split_hi(act, n + 3)
                    act.wait_ge(evac_sem[n % 3], use_of[n] + 1)
                    act.activation(pair(xbc, m), pair(xbc, m), ACT.Silu).then_inc(xbc_ready, 1)
                    if m % 3 == 2:
                        ya_part(m // 3)

                def decays(p):
                    act.wait_ge(row_mm, p + 1)
                    if p >= 2:
                        act.wait_ge(y_mm, p - 1)
                    for hh in range(2):
                        h, row = 2 * p + hh, s.bank[3 + p % 2][:, T * hh:T * hh + T]
                        for b, c in ((0, slice(0, P)), (1, slice(P, T)), (2, slice(P, T))):
                            own.add(act.activation(decay[:, p % 2, hh, P * b:P * b + P], row[:, c], ACT.Relu, scale=-1.0,
                                                   bias=shift[:, b, h:h + 1]))
                    own.wait()
                    both = decay[:, p % 2, :, :].rearrange("p h b -> p (h b)")
                    act.activation(both, both, ACT.Exp, scale=-1.0).then_inc(decay_ready, 1)

                def group_squares(g):
                    act.wait_ge(gated, g + 1)
                    for c in range(2):
                        act.activation(squares[c], pair(xbc, 2 * g + c), ACT.Square, scale=0.5).then_inc(squared, 1)
                    act.wait_ge(ms_mm, g + 1)
                    if g:
                        act.wait_ge(normed, g)
                    own.add(act.activation(rstd[:, :], s.bank[7][:, 0:T], ACT.Ln, bias=s.eps_ln))
                    own.wait()
                    act.activation(rstd[:, :], rstd[:, :], ACT.Exp, scale=-0.5).then_inc(rstd_ready, 1)

                def group_hi(g):
                    act.wait_ge(normed, g + 1)
                    if g == 2:
                        act.wait_ge(st.gemm_done, 44)
                    dst = ya_hi if g < 2 else u_hi
                    for i in range(4):
                        act.activation(dst[:, 4 * (g % 2) + i, :], xbc[:, 4 * g + i, :], ACT.Copy,
                                       scale=half_w[:, 4 * g + i:4 * g + i + 1]).then_inc(y_hi, 1)

                for n in range(24, 44):
                    if n >= 28:
                        decays(n - 28)
                    if n < 28:
                        evac(n, pair(gates, n - 24), ACT.Tanh, 0.5)
                    elif n < 32:
                        act.wait_ge(st.gemm_done, n + 1)
                    elif n < 40:
                        evac(n, pair(zt, n - 32), ACT.Tanh, 0.5, z_tanh)
                    else:
                        evac(n, pair(gates, n - 36), ACT.Tanh, 0.5)
                    split_hi(act, n + 3)
                    if n == 24:
                        act.wait_ge(acum_mm, 1)
                        for b, scale in ((0, 1.0), (1, -1.0), (2, 1.0)):
                            own.add(act.activation(shift[:, b, :], s.bank[7][:, 32 * b:32 * b + 32], ACT.Copy, scale=scale))
                        own.wait()
                        act.activation(acum_hi[:, :], s.bank[7][0:N_HEADS, P:P + T], ACT.Copy).then_inc(shift_ready, 1)
                    for g, at in ((0, 34), (1, 37), (2, 41)):
                        if n == at:
                            group_squares(g)
                        if n == at + 1 and g < 2:
                            group_hi(g)
                group_hi(2)
                group_squares(3)
                group_hi(3)
                for n in range(44, 56):
                    if n < 51:
                        split_hi(act, n + 3)
                    if 48 <= n < 52:
                        act.wait_ge(merged, n - 47)
                        act.activation(pair(ya_hi, n - 48), pair(gates, n - 44), ACT.Copy, scale=0.5).then_inc(merged_hi, 1)
                    if n >= 51:
                        split_hi(act, n + 3)

            @block.vector
            def _(dve):
                own = Count(dve, dve_own)
                step = own.add
                for t in range(TT):
                    for c in range(2):
                        step(dve.bn_stats(stats[:, t, c, :], s.h[:, t, 512 * c:512 * c + 512]))
                    own.wait()
                    step(dve.bn_aggr(mv[:, t, 0:2], stats[:, t, :, :].rearrange("p a c -> p (a c)")))
                    own.wait()
                    dve.scalar_tensor_tensor(out=mv[:, t, 2:3], in0=mv[:, t, 0:1], scalar=mv[:, t, 0:1], in1=mv[:, t, 1:2],
                                             op0=ALU.mult, op1=ALU.add).then_inc(var_ready, 1)
                step(dve.tensor_scalar(half_w[:, :], s.colrange("ssd_norm_w_2", 0, 16), 0.5, None, op0=ALU.mult))
                for t in range(TT):
                    dve.wait_ge(r_ready, t + 1)
                    dve.tensor_scalar(diag[:, t, :], C("identity"), mv[:, t, 4:5], None, op0=ALU.mult).then_inc(diag_ready, 1)
                split_lo(dve, 0)
                for k in range(KD):
                    dve.wait_ge(ut_hi, k + 1)
                    if k % 2 == 0:
                        dve.wait_ge(ut_hi, k + 2)
                    dve.scalar_tensor_tensor(out=u_lo[:, k, :], in0=s.bank[3 + k // 2][:, T * (k % 2):T * (k % 2) + T], scalar=s.col("norm_mix_w_2", k),
                                             in1=u_hi[:, k, :].bitcast(FP32), op0=ALU.mult, op1=ALU.subtract).then_inc(ut_lo, 1)
                for n in range(1, 3):
                    split_lo(dve, n)
                dve.wait_ge(dt_mm, 1)
                dve.wait_ge(par_loaded, 48)
                dve.tensor_tensor(dt[:, :, :], s.bank[7][:, 0:64].rearrange("p (t h) -> p t h", t=TT),
                                  dt_bias[:, :].unsqueeze(1).to_broadcast([P, TT, N_HEADS]), ALU.add).then_inc(dt_raw, 1)
                dve.wait_ge(dt_raw, 2)
                dve.scalar_tensor_tensor(out=dt[:, :, :], in0=dt[:, :, :], scalar=0.0, in1=dt_tmp[:, :, :], op0=ALU.max, op1=ALU.add).then_inc(dt_ready, 1)
                dve.wait_ge(dt_ready, 1)
                dve.scalar_tensor_tensor(out=loga[:, :, :], in0=dt[:, :, :], scalar=-1.0, in1=a_col[:, :].unsqueeze(1).to_broadcast([P, TT, N_HEADS]),
                                         op0=ALU.mult, op1=ALU.mult).then_inc(dt_ready, 1)
                for n in range(3, 15):
                    split_lo(dve, n)

                def conv_a_part(j):
                    dve.wait_ge(cv_ready, 4)
                    for d in range(A_TAPS):
                        for i in range(2):
                            f = 2 * j + i
                            w, x, o = s.col("conv_a_w_2", 8 * (A_TAPS - 1 - d) + f), bcv[:, 8 + f, :], bcv[:, 16 + f, :]
                            if d == 0:
                                step(dve.tensor_scalar(o, x, w, None, op0=ALU.mult))
                            else:
                                ins = dve.scalar_tensor_tensor(out=o[:, d:T], in0=x[:, 0:T - d], scalar=w, in1=o[:, d:T], op0=ALU.mult, op1=ALU.add)
                                if d == A_TAPS - 1 and i == 1:
                                    ins.then_inc(conv_a, 1)
                                else:
                                    step(ins)
                        own.wait()

                def ya_low(j):
                    dve.wait_ge(ya_hi_done, j + 1)
                    dve.tensor_tensor(pair(ya_lo, j), pair(bcv, j), pair(ya_hi, j).bitcast(FP32), ALU.subtract).then_inc(ya_done, 1)

                for n in range(12, 24):
                    m = n - 12
                    dve.wait_ge(tap_done, 2 * m + 2)
                    for d in range(1, XBC_TAPS):
                        for t in range(2):
                            f = 2 * m + t
                            o = xbc[:, f, d:T]
                            ins = dve.scalar_tensor_tensor(out=o, in0=s.bank[n % 3][:, T * t:T * t + T - d], scalar=s.col("ssd_conv_w_2", 24 * (3 - d) + f),
                                                           in1=o, op0=ALU.mult, op1=ALU.add)
                            if d == XBC_TAPS - 1 and t == 1:
                                ins.then_inc(evac_sem[n % 3], 1)
                            else:
                                step(ins)
                        own.wait()
                    split_lo(dve, n + 3)
                    if m % 3 == 0:
                        conv_a_part(m // 3)
                    if m >= 3 and m % 3 == 2:
                        ya_low(m // 3 - 1)

                def masked_cb(g):
                    dve.wait_ge(cb_mm, g + 1)
                    dve.wait_ge(cb_mm, 4)
                    src, dst = s.bank[3 + g], cbm[:, g, :]
                    step(dve.tensor_tensor(dst[:, 0:P], src[:, 0:P], C("causal"), ALU.mult))
                    step(dve.tensor_copy(dst[:, P:T], src[:, P:T]))
                    dve.tensor_tensor(dst[:, T:T + P], src[:, T:T + P], C("causal"), ALU.mult).then_inc(cbm_ready, 1)

                def x_tokens(f):
                    t, q = f // 4, f % 4
                    dve.wait_ge(xt_mm, f + 1)
                    dve.tensor_tensor(x_tok[:, t, 512 * q:512 * q + 512].rearrange("p (h d) -> p h d", d=64),
                                      s.bank[3 + f % 4][:, :].rearrange("p (h d) -> p h d", d=64),
                                      dt[:, t, 8 * q:8 * q + 8].unsqueeze(2).to_broadcast([P, 8, 64]), ALU.mult).then_inc(xtok_ready, 1)

                def weigh(p):
                    dve.wait_ge(decay_ready, p + 1)
                    m = decay[:, p % 2, :, :]
                    dve.tensor_tensor(m, m, cbm[:, p // 4, :].unsqueeze(1).to_broadcast([P, 2, 384]), ALU.mult).then_inc(m_ready, 1)

                def y_out(p):
                    dve.wait_ge(y_mm, p + 1)
                    dve.scalar_tensor_tensor(out=xbc[:, p, :], in0=xbc[:, p, :], scalar=s.cols[:, 0, p:p + 1], in1=s.bank[5 + p % 2][:, 0:T],
                                             op0=ALU.mult, op1=ALU.add).then_inc(y_ready, 1)

                def group_lo(g):
                    dst_hi, dst_lo = (ya_hi, ya_lo) if g < 2 else (u_hi, u_lo)
                    for i in range(4):
                        dve.wait_ge(y_hi, 4 * g + i + 1)
                        k = 4 * (g % 2) + i
                        dve.scalar_tensor_tensor(out=dst_lo[:, k, :], in0=xbc[:, 4 * g + i, :], scalar=half_w[:, 4 * g + i:4 * g + i + 1],
                                                 in1=dst_hi[:, k, :].bitcast(FP32), op0=ALU.mult, op1=ALU.subtract).then_inc(y_done, 1)

                for n in range(24, 44):
                    if n == 24:
                        ya_low(3)
                    if n == 25:
                        for g in range(4):
                            masked_cb(g)
                        dve.wait_ge(shift_ready, 1)
                        dve.tensor_tensor(acum_lo[:, :], s.bank[7][0:N_HEADS, P:P + T], acum_hi[:, :].bitcast(FP32), ALU.subtract).then_inc(shift_ready, 1)
                    if n in (26, 27):
                        for f in range(4):
                            x_tokens(4 * (n - 26) + f)
                    if n >= 28:
                        weigh(n - 28)
                        if n > 28:
                            y_out(n - 29)
                    b = bank_of[n]
                    if 28 <= n < 32:
                        g = pair(gates, n - 28)
                        dve.wait_ge(st.gemm_done, n + 1)
                        dve.scalar_tensor_tensor(out=g, in0=g, scalar=1.0, in1=s.bank[b][:, :], op0=ALU.add, op1=ALU.mult).then_inc(evac_sem[b], 1)
                    if 32 <= n < 40:
                        g = pair(zt, n - 32)
                        dve.wait_ge(z_tanh, n - 31)
                        dve.scalar_tensor_tensor(out=g, in0=g, scalar=1.0, in1=s.bank[b][:, :], op0=ALU.add, op1=ALU.mult).then_inc(evac_sem[b], 1)
                    split_lo(dve, n + 3)
                    for g, at in ((0, 36), (1, 39)):
                        if n == at:
                            group_lo(g)
                y_out(15)
                group_lo(2)
                group_lo(3)
                for n in range(44, 52):
                    if n >= 48:
                        cb, b = S_OUT[n - 44][0], bank_of[n]
                        g, a = pair(gates, 4 + cb), pair(gates, cb)
                        dve.wait_ge(st.gemm_done, n + 1)
                        dve.scalar_tensor_tensor(out=g, in0=g, scalar=1.0, in1=s.bank[b][:, :], op0=ALU.add, op1=ALU.mult).then_inc(evac_sem[b], 1)
                        dve.wait_ge(evac_sem[b], use_of[n] + 1)
                        dve.tensor_tensor(g, g, a, ALU.add).then_inc(merged, 1)
                        dve.wait_ge(merged_hi, cb + 1)
                        dve.scalar_tensor_tensor(out=pair(ya_lo, cb), in0=g, scalar=0.5, in1=pair(ya_hi, cb).bitcast(FP32),
                                                 op0=ALU.mult, op1=ALU.subtract).then_inc(merged_done, 1)
                    split_lo(dve, n + 3)
                for n in range(52, 56):
                    split_lo(dve, n + 3)
                for c in range(4):
                    n = 52 + c
                    hc = s.h[:, :, COLS * c:COLS * c + COLS]
                    dve.wait_ge(st.gemm_done, n + 1)
                    dve.tensor_tensor(hc, hc, s.bank[bank_of[n]][:, :].rearrange("p (a n) -> p a n", a=2), ALU.add).then_inc(evac_sem[bank_of[n]], 1)

            @block.tensor
            def _(pe):
                pe.wait_ge(diag_ready, 2)
                for c in range(4):
                    for i in range(4):
                        k, t = 2 * c + i // 2, i % 2
                        m = pe.matmul(s.bank[3 + c][:, P * i:P * i + P], lhsT=s.h[:, t, k * P:k * P + P], rhs=diag[:, t, :], start=True, stop=True)
                    m.then_inc(ut_mm, 1)
                pe.wait_ge(ut_lo, KD)

                def gemm(q, i, bank, x, tokens=False, first=True, last=True, used=None):
                    pe.wait_ge(st.lo_done, q * 3 + i + 1)
                    if first and not (isinstance(used, int) and used == 0):
                        pe.wait_ge(evac_sem[bank], used)
                    w = st.w(i, KD, COLS)
                    if tokens:
                        def merged_part(part, k):
                            if part == 0:
                                pe.wait_ge(merged_done, k // 2 + 1)
                            return x[part][:, k, :]
                        m = tokens_out(pe, s.bank[bank], w, None, KD, merged_part)
                    else:
                        m = features_out(pe, s.bank[bank], w, x, 0, KD, first, last)
                    m.then_inc(st.gemm_done, 1)

                def unit(n, x, **kw):
                    gemm(n // 3, n % 3, bank_of[n], x, used=use_of[n], **kw)

                u, ya = (u_hi, u_lo), (ya_hi, ya_lo)
                unit(0, u)
                pe.wait_ge(par_loaded, 48)
                for t in range(TT):
                    for k in range(KD):
                        for x in (u_hi, u_lo):
                            m = pe.matmul(s.bank[7][:, 32 * t:32 * t + 32], lhsT=x[:, k, P * t:P * t + P].bitcast(FP32), rhs=w_dt[:, k, :],
                                          start=(k == 0 and x is u_hi), stop=(k == KD - 1 and x is u_lo))
                m.then_inc(dt_mm, 1)
                unit(1, u)
                unit(2, u)
                with pe.Fori(1, 8) as q:
                    for i in range(3):
                        gemm(q, i, i, u, used=q)

                def row_sums(p):
                    if p >= 2:
                        pe.wait_ge(decay_ready, p - 1)
                    for hh in range(2):
                        h = 2 * p + hh
                        out, head = s.bank[3 + p % 2][:, T * hh:T * hh + T], pick[:, h:h + 1].to_broadcast([N_HEADS, P])
                        pe.matmul(out, lhsT=head, rhs=acum_hi[:, :], start=True, stop=False)
                        m = pe.matmul(out, lhsT=head, rhs=acum_lo[:, :], start=False, stop=True)
                    m.then_inc(row_mm, 1)

                def scan_out(p):
                    pe.wait_ge(m_ready, p + 1)
                    if p >= 2:
                        pe.wait_ge(y_ready, p - 1)
                    for hh in range(2):
                        r, f = slice(64 * hh, 64 * hh + 64), slice(64 * (2 * p + hh), 64 * (2 * p + hh) + 64)
                        bank, w = s.bank[5 + p % 2], decay[:, p % 2, hh, :]
                        pe.matmul(bank[r, 0:T], lhsT=x_tok[:, 0, f], rhs=w[:, 0:T], start=True, stop=False)
                        m = pe.matmul(bank[r, P:T], lhsT=x_tok[:, 1, f], rhs=w[:, T:T + P], start=False, stop=True)
                    m.then_inc(y_mm, 1)

                def mean_squares(g):
                    pe.wait_ge(squared, 2 * g + 2)
                    for i in range(4):
                        m = pe.matmul(s.bank[7][:, 0:T], lhsT=C("mean512"), rhs=squares[i // 2][:, T * (i % 2):T * (i % 2) + T], start=(i == 0), stop=(i == 3))
                    m.then_inc(ms_mm, 1)

                for n in range(24, 28):
                    unit(n, u)
                    if n == 24:
                        pe.wait_ge(dt_ready, 2)
                        pe.matmul(s.bank[7][:, 0:32], lhsT=C("causal"), rhs=loga[:, 0, :], start=True, stop=True)
                        pe.matmul(s.bank[7][:, 32:64], lhsT=C("strict_lower"), rhs=loga[:, 0, :], start=True, stop=True)
                        pe.matmul(s.bank[7][:, 64:96], lhsT=C("causal"), rhs=loga[:, 1, :], start=True, stop=True)
                        for t in range(TT):
                            m = pe.matmul(s.bank[7][0:N_HEADS, P + P * t:2 * P + P * t], lhsT=loga[:, t, :], rhs=C("causal"), start=True, stop=True)
                        m.then_inc(acum_mm, 1)
                    if n == 25:
                        pe.wait_ge(xbc_ready, 12)
                        for g in range(N_GROUPS):
                            b_t, c_t = xbc[:, 16 + g, :], xbc[:, 20 + g, :]
                            pe.matmul(s.bank[3 + g][:, 0:T], lhsT=b_t[:, 0:P], rhs=c_t, start=True, stop=True)
                            pe.matmul(s.bank[3 + g][:, T:T + P], lhsT=b_t[:, P:T], rhs=c_t[:, P:T], start=True, stop=True).then_inc(cb_mm, 1)
                    if n in (26, 27):
                        for f in range(4 * (n - 26), 4 * (n - 26) + 4):
                            pe.wait_ge(cbm_ready, f + 1) if f < 4 else pe.wait_ge(xtok_ready, f - 3)
                            if f == 0:
                                pe.wait_ge(ya_done, 4)
                            t, q = f // 4, f % 4
                            for i in range(4):
                                m = pe.transpose(s.bank[3 + f % 4][:, P * i:P * i + P], xbc[:, 4 * q + i, P * t:P * t + P], C("identity"))
                            m.then_inc(xt_mm, 1)
                pe.wait_ge(xtok_ready, 8)
                pe.wait_ge(shift_ready, 2)
                row_sums(0)
                for n in range(28, 44):
                    if n + 1 < 44:
                        row_sums(n - 27)
                    unit(n, ya if n < 32 else u)
                    scan_out(n - 28)
                    for g, at in ((0, 34), (1, 37), (2, 41)):
                        if n == at:
                            mean_squares(g)
                pe.wait_ge(y_done, 8)
                for n in range(44, 48):
                    if n == 45:
                        mean_squares(3)
                    if n == 47:
                        pe.wait_ge(decay_ready, 16)
                    unit(n, ya, last=False)
                pe.wait_ge(y_done, 16)
                for n in range(48, 52):
                    unit(n, u, first=False)
                for n in range(52, 56):
                    unit(n, ya, tokens=True)
        nc.clear_and_free_semaphores(sems)
        nc.all_engine_barrier()


def ffn(nc, A, s):
    D_FF, TAPS = 2816, 3
    KF = D_FF // P
    UP_UNITS, DOWN_K = 2 * D_FF // COLS, (8, 8, 6)
    N_UNITS = UP_UNITS + 4 * len(DOWN_K)
    with ExitStack() as ctx:
        def sb(name, shape, dt=FP32):
            return ctx.enter_context(nc.sbuf_tensor(name, shape, dt))

        sems = []

        def sem(name):
            sems.append(nc.alloc_semaphore(name))
            return sems[-1]

        s.w_hi = sb("m4_w_hi", [P, RING, KD * COLS], F32R)
        s.w_lo = sb("m4_w_lo", [P, RING, KD * COLS], F32R)
        v_hi, v_lo = sb("v_hi", [P, KD, T], F32R), sb("v_lo", [P, KD, T], F32R)
        h1 = sb("h1", [P, KF, T])
        prod = sb("h1_h3", [P, 2, 2, T])
        p_hi, p_lo = sb("p_hi", [P, KF, T], F32R), sb("p_lo", [P, KF, T], F32R)
        fw = sb("final_norm_w", [P, D])
        stats, mv = sb("rms4_stats", [P, TT, 2, 6]), sb("rms4_mv", [P, 2 * TT, 5])
        diag = sb("diag4", [P, TT, P])
        C = lambda name: s.con[:, SHARED.index(name), :]
        st = Stream(s, sem, "m4")
        evac_sem = [sem(f"m4_evac{i}") for i in range(4)]
        (fw_loaded, var_ready, r_ready, diag_ready, vt_mm, vt_hi, vt_lo, tap_done, h1_ready, p_ready, p_hi_done, p_done,
         act_own, dve_own, out_ready, stored) = (sem("m4_" + n) for n in (
            "fw_loaded", "var_ready", "r_ready", "diag_ready", "vt_mm", "vt_hi", "vt_lo", "tap_done", "h1_ready", "p_ready",
            "p_hi_done", "p_done", "act_own", "dve_own", "out_ready", "stored"))

        DOWN = [(c, k) for c in range(4) for k in range(len(DOWN_K))]

        def size(n):
            return (KD if n < UP_UNITS else DOWN_K[DOWN[n - UP_UNITS][1]]) * COLS

        def split_hi(act, n):
            if n < N_UNITS:
                st.hi(act, n // 3, n % 3, size(n), n - 2 if n >= 3 else None)

        def split_lo(dve, n):
            if n < N_UNITS:
                st.lo(dve, n // 3, n % 3, size(n))

        def pair(t, c):
            return t[:, 2 * c:2 * c + 2, :].rearrange("p a t -> p (a t)")

        def rms(eng_dve, own, base, t):
            for c in range(2):
                own.add(eng_dve.bn_stats(stats[:, t, c, :], s.h[:, t, 512 * c:512 * c + 512]))
            own.wait()
            own.add(eng_dve.bn_aggr(mv[:, base + t, 0:2], stats[:, t, :, :].rearrange("p a c -> p (a c)")))
            own.wait()
            m = mv[:, base + t, :]
            eng_dve.scalar_tensor_tensor(out=m[:, 2:3], in0=m[:, 0:1], scalar=m[:, 0:1], in1=m[:, 1:2], op0=ALU.mult, op1=ALU.add).then_inc(var_ready, 1)

        with nc.Block() as block:
            @block.sync
            def _(sp):
                w_up = A["w_up_2"][0].rearrange("(k p) n -> p k n", p=P)
                w_down = A["w_down_2"][0].rearrange("(k p) n -> p k n", p=P)
                for n in range(3, N_UNITS):
                    if n < UP_UNITS:
                        st.load(sp, n // 3, n % 3, w_up[:, :, COLS * n:COLS * n + COLS], KD, COLS)
                    else:
                        c, k = DOWN[n - UP_UNITS]
                        st.load(sp, n // 3, n % 3, w_down[:, 8 * k:8 * k + DOWN_K[k], COLS * c:COLS * c + COLS], DOWN_K[k], COLS)
                for t in range(TT):
                    sp.wait_ge(out_ready, t + 1)
                    sp.dma_start(s.out[0, P * t:P * t + P, :], s.h[:, t, :]).then_inc(stored, 16)
                sp.wait_ge(stored, 32)

            @block.gpsimd
            def _(pool):
                pool.dma_start(fw[:, :], A["final_norm_w_2"].partition_broadcast(P)).then_inc(fw_loaded, 16)

            @block.scalar
            def _(act):
                own = Count(act, act_own)

                def inverse_rms(j):
                    act.wait_ge(var_ready, j + 1)
                    own.add(act.activation(mv[:, j, 3:4], mv[:, j, 2:3], ACT.Ln, bias=s.eps_ln))
                    own.wait()
                    act.activation(mv[:, j, 4:5], mv[:, j, 3:4], ACT.Exp, scale=-0.5).then_inc(r_ready, 1)

                split_hi(act, 0)
                for t in range(TT):
                    inverse_rms(t)
                for k in range(KD):
                    act.wait_ge(vt_mm, k // 2 + 1)
                    act.activation(v_hi[:, k, :], s.bank[4 + k // 2][:, T * (k % 2):T * (k % 2) + T], ACT.Copy, scale=s.col("norm_ffn_w_2", k)).then_inc(vt_hi, 1)
                    if k % 4 == 3:
                        split_hi(act, 1 + k // 4)
                for n in range(UP_UNITS):
                    act.wait_ge(st.gemm_done, n + 1)
                    if n < UP_UNITS // 2:
                        for t in range(2):
                            f = 2 * n + t
                            act.activation(h1[:, f, :], s.bank[n % 3][:, T * t:T * t + T], ACT.Identity,
                                           scale=s.col("ffn_conv_w_2", KF * (TAPS - 1) + f), bias=s.col("ffn_conv_b_2", f)).then_inc(tap_done, 1)
                        split_hi(act, n + 3)
                        act.wait_ge(evac_sem[n % 3], n // 3 + 1)
                        act.activation(pair(h1, n), pair(h1, n), ACT.Silu).then_inc(h1_ready, 1)
                    else:
                        c = n - UP_UNITS // 2
                        split_hi(act, n + 3)
                        act.wait_ge(p_ready, c + 1)
                        act.activation(pair(p_hi, c), prod[:, c % 2, :, :].rearrange("p a t -> p (a t)"), ACT.Copy).then_inc(p_hi_done, 1)
                for n in range(UP_UNITS, N_UNITS):
                    split_hi(act, n + 3)
                for t in range(TT):
                    inverse_rms(TT + t)

            @block.vector
            def _(dve):
                own = Count(dve, dve_own)
                for t in range(TT):
                    rms(dve, own, 0, t)
                for t in range(TT):
                    dve.wait_ge(r_ready, t + 1)
                    dve.tensor_scalar(diag[:, t, :], C("identity"), mv[:, t, 4:5], None, op0=ALU.mult).then_inc(diag_ready, 1)
                split_lo(dve, 0)
                for k in range(KD):
                    dve.wait_ge(vt_hi, 2 * (k // 2) + 2)
                    dve.scalar_tensor_tensor(out=v_lo[:, k, :], in0=s.bank[4 + k // 2][:, T * (k % 2):T * (k % 2) + T], scalar=s.col("norm_ffn_w_2", k),
                                             in1=v_hi[:, k, :].bitcast(FP32), op0=ALU.mult, op1=ALU.subtract).then_inc(vt_lo, 1)
                for n in range(1, 3):
                    split_lo(dve, n)
                for n in range(UP_UNITS):
                    if n < UP_UNITS // 2:
                        dve.wait_ge(tap_done, 2 * n + 2)
                        for d in range(1, TAPS):
                            for t in range(2):
                                f = 2 * n + t
                                o = h1[:, f, d:T]
                                ins = dve.scalar_tensor_tensor(out=o, in0=s.bank[n % 3][:, T * t:T * t + T - d], scalar=s.col("ffn_conv_w_2", KF * (TAPS - 1 - d) + f),
                                                               in1=o, op0=ALU.mult, op1=ALU.add)
                                if d == TAPS - 1 and t == 1:
                                    ins.then_inc(evac_sem[n % 3], 1)
                                else:
                                    own.add(ins)
                            own.wait()
                    else:
                        c = n - UP_UNITS // 2
                        dve.wait_ge(st.gemm_done, n + 1)
                        dve.wait_ge(h1_ready, c + 1)
                        if c >= 2:
                            dve.wait_ge(p_hi_done, c - 1)
                        pr = prod[:, c % 2, :, :].rearrange("p a t -> p (a t)")
                        dve.tensor_tensor(pr, s.bank[n % 3][:, :], pair(h1, c), ALU.mult).then_inc(p_ready, 1)
                        dve.wait_ge(p_ready, c + 1)
                        dve.wait_ge(p_hi_done, c + 1)
                        dve.tensor_tensor(pair(p_lo, c), pr, pair(p_hi, c).bitcast(FP32), ALU.subtract).then_inc(evac_sem[n % 3], 1)
                    split_lo(dve, n + 3)
                for n in range(UP_UNITS, N_UNITS):
                    split_lo(dve, n + 3)
                    c, k = DOWN[n - UP_UNITS]
                    if k == len(DOWN_K) - 1:
                        hc = s.h[:, :, COLS * c:COLS * c + COLS]
                        dve.wait_ge(st.gemm_done, n + 1)
                        dve.tensor_tensor(hc, hc, s.bank[4 + c][:, :].rearrange("p (a n) -> p a n", a=2), ALU.add).then_inc(evac_sem[3], 1)
                dve.wait_ge(evac_sem[3], 4)
                for t in range(TT):
                    rms(dve, own, TT, t)
                dve.wait_ge(fw_loaded, 16)
                for t in range(TT):
                    dve.wait_ge(r_ready, TT + t + 1)
                    dve.scalar_tensor_tensor(out=s.h[:, t, :], in0=s.h[:, t, :], scalar=mv[:, TT + t, 4:5], in1=fw[:, :],
                                             op0=ALU.mult, op1=ALU.mult).then_inc(out_ready, 1)

            @block.tensor
            def _(pe):
                pe.wait_ge(diag_ready, 2)
                for c in range(4):
                    for i in range(4):
                        k, t = 2 * c + i // 2, i % 2
                        m = pe.matmul(s.bank[4 + c][:, P * i:P * i + P], lhsT=s.h[:, t, k * P:k * P + P], rhs=diag[:, t, :], start=True, stop=True)
                    m.then_inc(vt_mm, 1)
                pe.wait_ge(vt_lo, KD)
                v = (v_hi, v_lo)

                def up(q, i, used):
                    pe.wait_ge(st.lo_done, q * 3 + i + 1)
                    if not (isinstance(used, int) and used == 0):
                        pe.wait_ge(evac_sem[i], used)
                    features_out(pe, s.bank[i], st.w(i, KD, COLS), v, 0, KD).then_inc(st.gemm_done, 1)

                for i in range(3):
                    up(0, i, 0)
                with pe.Fori(1, UP_UNITS // 3) as q:
                    for i in range(3):
                        up(q, i, q)
                up(UP_UNITS // 3, 0, UP_UNITS // 3)
                pe.wait_ge(evac_sem[(UP_UNITS - 1) % 3], (UP_UNITS - 1) // 3 + 1)
                for n in range(UP_UNITS, N_UNITS):
                    c, kk = DOWN[n - UP_UNITS]
                    pe.wait_ge(st.lo_done, n + 1)
                    w = st.w(n % 3, DOWN_K[kk], COLS)
                    for t in range(TT):
                        for k in range(DOWN_K[kk]):
                            f, tok = 8 * kk + k, slice(P * t, P * t + P)
                            m = product3(pe, s.bank[4 + c][:, COLS * t:COLS * t + COLS], (p_hi[:, f, tok], p_lo[:, f, tok]),
                                         (w[0][:, k, :], w[1][:, k, :]), kk + t + k == 0, kk == len(DOWN_K) - 1 and k == DOWN_K[kk] - 1, True)
                    m.then_inc(st.gemm_done, 1)


def whole_block(nc, A, out, phases):
    with ExitStack() as ctx:
        def sb(name, shape, dt=FP32):
            return ctx.enter_context(nc.sbuf_tensor(name, shape, dt))

        s = Shared()
        s.bank = [ctx.enter_context(nc.psum_tensor(f"bank{i}", [P, 512], FP32)) for i in range(8)]
        s.raw = sb("raw_weights", [P, RING, KD * COLS])
        s.h = sb("hidden", [P, TT, D])
        s.con = sb("shared_constants", [P, len(SHARED), P])
        s.rows, s.cols = sb("parameter_rows", [P, 3, P]), sb("parameter_cols", [P, 3, P])
        s.dskip = sb("d_skip_pairs", [16, 2])
        s.eps = sb("eps", [P, 4])
        s.eps_ln, s.eps_hg = s.eps[:, 0:1], s.eps[:, 1:2]
        s.gate = sb("expert_gates", [P, TT, N_EXPERTS])
        s.slot = sb("expert_slots", [P, TT, PASSES * N_EXPERTS + 1])
        s.n_steps = sb("n_steps", [1, 1], INT32)
        s.row_map = {"norm_mix_w_2": (0, 32, 8), "ssd_norm_w_2": (0, 40, 16), "conv_a_w_2": (0, 56, 24),
                     "ssd_conv_b_2": (0, 80, 24), "hgrn_lb_logits": (0, 104, 8), "hgrn_norm_g": (0, 112, 4),
                     "ssd_conv_w_2": (1, 0, 96), "norm_ffn_w_2": (2, 0, 8), "ffn_conv_w_2": (2, 8, 66),
                     "ffn_conv_b_2": (2, 74, 22)}

        def colrange(name, i, n):
            tile, r, _ = s.row_map[name]
            return s.cols[:, tile, r + i:r + i + n]
        s.colrange = colrange
        s.col = lambda name, i: colrange(name, i, 1)
        s.out = out
        s.raw_full = {name: [nc.alloc_semaphore(f"{name}_raw_full{i}") for i in range(RING)] for name in ("m1", "m3", "m4")}
        s.expert_full = [nc.alloc_semaphore(f"expert_unit{u}_full") for u in range(EXPERT_UNITS)]

        def load_expert_unit(sp, u, e):
            name, c = ("expert_w_up", u) if u < 4 else ("expert_w_down", u - 4)
            w = A[name][0].rearrange("e (k p) n -> e p k n", p=P)[bass.ds(e, 1), :, :, 512 * c:512 * c + 512]
            sp.dma_start(s.expert_units[u], w.rearrange("o p k n -> (o p) k n")).then_inc(s.expert_full[u], 16)
        s.load_expert_unit = load_expert_unit

        def load_first(sp, name, i):
            source, c0 = {"m3": ("w_in_2", 2 * D), "m4": ("w_up_2", 0)}[name]
            w = A[source][0].rearrange("(k p) n -> p k n", p=P)[:, :, c0 + COLS * i:c0 + COLS * i + COLS]
            sp.dma_start(s.raw[:, i, :].rearrange("p (k n) -> p k n", k=KD), w).then_inc(s.raw_full[name][i], 16)
        s.load_first = load_first
        with nc.sbuf_tensor("expert_weights", [P, 3, KD * 512], FP32) as s.expert_weights, \
                nc.sbuf_tensor("bias_rows", [P, 2, 256], FP32) as s.bias_rows, \
                nc.sbuf_tensor("bias_t", [P, N_EXPERTS, 2, KD], FP32) as s.bias_t, \
                nc.sbuf_tensor("b_down", [N_EXPERTS, D], FP32) as s.b_down:
            units = [s.raw[:, 0:2, :].rearrange("p a n -> p (a n)")] + [s.expert_weights[:, u, :] for u in range(3)]
            s.expert_units = [w.rearrange("p (k n) -> p k n", k=KD) for w in units]
            with nc.sbuf_tensor("expert_weights_late", [P, 2, KD * 512], FP32) as late:
                s.expert_units += [late[:, i, :].rearrange("p (k n) -> p k n", k=KD) for i in range(2)]
            for phase in phases[0:2]:
                phase(nc, A, s)
        for phase in phases[2:]:
            phase(nc, A, s)
        if ffn in phases:
            return
        stored = ctx.enter_context(nc.semaphore("stored"))
        with nc.Block() as block:
            @block.sync
            def _(sp):
                sp.dma_start(out[0].rearrange("(a p) d -> p a d", p=P), s.h[:, :, :]).then_inc(stored, 16)
                sp.wait_ge(stored, 16)


_OUTS = [((1, 256, 1024), "float32")]


def kernel(**inputs):
    import numpy as _np
    import concourse.bacc as _bacc
    from concourse import mybir as _mybir
    from concourse.bass_utils import run_bass_kernel_spmd as _run

    nc = _bacc.Bacc("TRN2", target_bir_lowering=False, num_devices=1)
    arrays, args = {}, {}
    for name, value in {**inputs, "constants": shape_constants()}.items():
        a = _np.ascontiguousarray(value)
        arrays[f"in_{name}_dram"] = a
        args[name] = nc.dram_tensor(f"in_{name}_dram", a.shape, _mybir.dt.from_np(a.dtype), kind="ExternalInput").ap()
    outs = [nc.dram_tensor(f"out_{i}_dram", shape, _mybir.dt.from_np(_np.dtype(dtype)), kind="ExternalOutput").ap()
            for i, (shape, dtype) in enumerate(_OUTS)]
    whole_block(nc, args, outs[0], PHASES)
    r = _run(nc, [arrays], core_ids=[0])
    return r.results[0]["out_0_dram"]


PHASES = (mixer1, experts, mixer2, ffn)
```
